# Optimizing a Trainium2 kernel written in Bass

```python
import math
import jax, jax.numpy as jnp
from jax import lax
import numpy as np
import jax
import jax.numpy as jnp

D_MODEL = 1024
BATCH = 1
SEQ = 256
DEPTH = 1

HEAD_DIM = 64
DILATED_GROUPS = ((128, 1), (512, 4), (2048, 16))
N_DIL = len(DILATED_GROUPS)
HEADS_PER_GROUP = 8
N_ATTN_HEADS = N_DIL * HEADS_PER_GROUP
ATTN_WIDTH = N_ATTN_HEADS * HEAD_DIM
ATTN_OUT_WIDTH = HEADS_PER_GROUP * HEAD_DIM
ATTN_BLOCK = 128
N_REL_BUCKETS = 32
REL_MAX_DISTANCE = 2048

D_INNER = 2 * D_MODEL
SSM_HEAD_DIM = 64
N_SSM_HEADS = D_INNER // SSM_HEAD_DIM
N_SSM_GROUPS = 4
HEADS_PER_SSM_GROUP = N_SSM_HEADS // N_SSM_GROUPS
D_STATE = 128
CONV_WIDTH = 4
SSD_CHUNK = 128
XBC_WIDTH = D_INNER + 2 * N_SSM_GROUPS * D_STATE

N_BRANCHES = 2
D_FF = -(-8 * D_MODEL // (3 * 256)) * 256
IN_PROJ_WIDTH = 3 * ATTN_WIDTH + D_INNER + XBC_WIDTH + N_SSM_HEADS + N_BRANCHES * D_MODEL
EPS = 1e-6


def rmsnorm(x, w):
    xf = x.astype(jnp.float32)
    y = xf * lax.rsqrt(jnp.mean(xf * xf, axis=-1, keepdims=True) + EPS)
    return (y * w.astype(jnp.float32)).astype(x.dtype)

def t5_causal_bucket(dist):
    max_exact = N_REL_BUCKETS // 2
    d_f = jnp.maximum(dist, 1).astype(jnp.float32)
    large = max_exact + (jnp.log(d_f / max_exact) / math.log(REL_MAX_DISTANCE / max_exact)
                         * (N_REL_BUCKETS - max_exact)).astype(jnp.int32)
    large = jnp.minimum(large, N_REL_BUCKETS - 1)
    return jnp.where(dist < max_exact, dist, large)

def rel_bias_block(rel_bias_g, dilation, n_steps):
    qi = jnp.arange(ATTN_BLOCK)[:, None]
    kj = jnp.arange(2 * ATTN_BLOCK)[None, :]
    steps = jnp.clip(qi + ATTN_BLOCK - kj, 0, n_steps)
    bucket = t5_causal_bucket(steps * dilation)
    return jnp.transpose(rel_bias_g[bucket], (2, 0, 1)).astype(jnp.float32)

def dilated_window_attention(q, k, v, bias, dilation, n_steps):
    b, s, h, dh = q.shape
    seg = s // dilation
    nb = -(-seg // ATTN_BLOCK)
    segp = nb * ATTN_BLOCK

    def to_blocks(t):
        t = t.reshape(b, seg, dilation, h, dh).transpose(0, 2, 1, 3, 4).reshape(b * dilation, seg, h, dh)
        t = jnp.pad(t, ((0, 0), (0, segp - seg), (0, 0), (0, 0)))
        return t.reshape(b * dilation, nb, ATTN_BLOCK, h, dh)

    def with_prev(t):
        prev = jnp.pad(t[:, :-1], ((0, 0), (1, 0), (0, 0), (0, 0), (0, 0)))
        return jnp.concatenate([prev, t], axis=2)

    qb = to_blocks(q)
    kw = with_prev(to_blocks(k))
    vw = with_prev(to_blocks(v))

    qi = jnp.arange(ATTN_BLOCK)[:, None]
    kj = jnp.arange(2 * ATTN_BLOCK)[None, :]
    steps = qi + ATTN_BLOCK - kj
    blk = jnp.arange(nb)[:, None, None]
    valid = (steps >= 0) & (steps <= n_steps) & (blk * ATTN_BLOCK - ATTN_BLOCK + kj >= 0)

    logits = jnp.einsum('znqhd,znkhd->znhqk', qb, kw).astype(jnp.float32) * (HEAD_DIM ** -0.5) + bias
    logits = jnp.where(valid[None, :, None], logits, -jnp.inf)
    m = jnp.max(logits, axis=-1, keepdims=True)
    p = jnp.exp(logits - m)
    den = jnp.sum(p, axis=-1, keepdims=True)
    o = jnp.einsum('znhqk,znkhd->znqhd', p, vw.astype(jnp.float32)) / jnp.swapaxes(den, 2, 3)
    lse = jnp.swapaxes((m + jnp.log(den))[..., 0], 2, 3)

    o = o.reshape(b, dilation, segp, h, dh)[:, :, :seg]
    o = jnp.swapaxes(o, 1, 2).reshape(b, s, h, dh)
    lse = lse.reshape(b, dilation, segp, h)[:, :, :seg]
    lse = jnp.swapaxes(lse, 1, 2).reshape(b, s, h)
    return o, lse

def causal_depthwise_conv(x, w, bias):
    c = x.shape[-1]
    y = lax.conv_general_dilated(x, w[:, None, :], window_strides=(1,),
                                 padding=((CONV_WIDTH - 1, 0),),
                                 dimension_numbers=('NWC', 'WIO', 'NWC'),
                                 feature_group_count=c)
    return y + bias

def ssd_chunked_scan(xh, dt, a, bm, cm):
    b, s = xh.shape[:2]
    nc = s // SSD_CHUNK

    def chunks(t):
        return jnp.swapaxes(t.reshape(b, nc, SSD_CHUNK, *t.shape[2:]), 0, 1)

    causal = jnp.tril(jnp.ones((SSD_CHUNK, SSD_CHUNK), dtype=bool))[None, :, :, None, None]

    def step(state, inp):
        x_, dt_, b_, c_ = inp
        la = jnp.cumsum(dt_ * a, axis=1)
        seg = la[:, :, None] - la[:, None, :]
        decay = jnp.exp(jnp.where(causal, seg, -jnp.inf))
        cb = jnp.einsum('bign,bjgn->bijg', c_, b_)
        xdt = x_ * dt_[..., None]
        y_intra = jnp.einsum('bijg,bijgh,bjghp->bighp', cb, decay, xdt)
        y_inter = jnp.einsum('bign,bghpn->bighp', c_, state) * jnp.exp(la)[..., None]
        to_end = jnp.exp(la[:, -1:] - la)
        new_state = (state * jnp.exp(la[:, -1])[..., None, None]
                     + jnp.einsum('bjgn,bjgh,bjghp->bghpn', b_, to_end, xdt))
        return new_state, y_intra + y_inter

    state0 = jnp.zeros((b, N_SSM_GROUPS, HEADS_PER_SSM_GROUP, SSM_HEAD_DIM, D_STATE), jnp.float32)
    _, ys = lax.scan(step, state0, (chunks(xh), chunks(dt), chunks(bm), chunks(cm)))
    return jnp.swapaxes(ys, 0, 1).reshape(b, s, N_SSM_GROUPS, HEADS_PER_SSM_GROUP, SSM_HEAD_DIM)

def hybrid_mixer(xn, w_in, conv_w, conv_b, dt_bias, a_log, d_skip, ssm_norm_w,
                 w_attn_branch, w_ssm_branch, w_out, attn_biases):
    b, s, _ = xn.shape
    proj = xn @ w_in
    q, k, v, z, xbc, dt_raw, gate_logits = jnp.split(
        proj, np.cumsum([ATTN_WIDTH, ATTN_WIDTH, ATTN_WIDTH, D_INNER, XBC_WIDTH, N_SSM_HEADS]).tolist(), axis=-1)

    q = q.reshape(b, s, N_DIL, HEADS_PER_GROUP, HEAD_DIM)
    k = k.reshape(b, s, N_DIL, HEADS_PER_GROUP, HEAD_DIM)
    v = v.reshape(b, s, N_DIL, HEADS_PER_GROUP, HEAD_DIM)
    outs, lses = [], []
    for g, (window, dil) in enumerate(DILATED_GROUPS):
        o_g, lse_g = dilated_window_attention(q[:, :, g], k[:, :, g], v[:, :, g],
                                              attn_biases[g], dil, window // dil)
        outs.append(o_g)
        lses.append(lse_g)
    o = jnp.stack(outs, axis=2)
    alpha = jax.nn.softmax(jnp.stack(lses, axis=2), axis=2)
    attn = jnp.sum(alpha[..., None] * o, axis=2).reshape(b, s, ATTN_OUT_WIDTH).astype(xn.dtype)

    xbc = jax.nn.silu(causal_depthwise_conv(xbc, conv_w, conv_b))
    xs, bm, cm = jnp.split(xbc, [D_INNER, D_INNER + N_SSM_GROUPS * D_STATE], axis=-1)
    xh = xs.reshape(b, s, N_SSM_GROUPS, HEADS_PER_SSM_GROUP, SSM_HEAD_DIM).astype(jnp.float32)
    bm = bm.reshape(b, s, N_SSM_GROUPS, D_STATE).astype(jnp.float32)
    cm = cm.reshape(b, s, N_SSM_GROUPS, D_STATE).astype(jnp.float32)
    dt = jax.nn.softplus(dt_raw.astype(jnp.float32) + dt_bias.astype(jnp.float32))
    dt = dt.reshape(b, s, N_SSM_GROUPS, HEADS_PER_SSM_GROUP)
    a = -jnp.exp(a_log.astype(jnp.float32)).reshape(N_SSM_GROUPS, HEADS_PER_SSM_GROUP)
    y = ssd_chunked_scan(xh, dt, a, bm, cm)
    y = y + xh * d_skip.astype(jnp.float32).reshape(N_SSM_GROUPS, HEADS_PER_SSM_GROUP)[..., None]
    yg = (y.reshape(b, s, D_INNER) * jax.nn.silu(z.astype(jnp.float32))).reshape(b, s, N_SSM_GROUPS, D_INNER // N_SSM_GROUPS)
    yg = yg * lax.rsqrt(jnp.mean(yg * yg, axis=-1, keepdims=True) + EPS)
    ssm = (yg.reshape(b, s, D_INNER) * ssm_norm_w.astype(jnp.float32)).astype(xn.dtype)

    gates = jax.nn.sigmoid(gate_logits.astype(jnp.float32)).reshape(b, s, N_BRANCHES, D_MODEL)
    merged = (gates[:, :, 0] * (attn @ w_attn_branch).astype(jnp.float32)
              + gates[:, :, 1] * (ssm @ w_ssm_branch).astype(jnp.float32)).astype(xn.dtype)
    return merged @ w_out

def swiglu(xn, w_ffn_in, w_ffn_out):
    gate, up = jnp.split(xn @ w_ffn_in, 2, axis=-1)
    return (jax.nn.silu(gate) * up) @ w_ffn_out

def first_inputs(seed: int = 0) -> dict:
    key = jax.random.key(seed)
    ks = jax.random.split(key, 20)
    f32 = jnp.float32
    nrm = lambda k, shape, scale: jax.random.normal(k, shape, f32) * scale
    dt0 = jnp.exp(jax.random.uniform(ks[5], (DEPTH, N_SSM_HEADS), f32, math.log(1e-3), math.log(1e-1)))
    return {
        "x": nrm(ks[0], (BATCH, SEQ, D_MODEL), 1.0),
        "norm1_w": 1.0 + nrm(ks[1], (DEPTH, D_MODEL), 0.02),
        "w_in": nrm(ks[2], (DEPTH, D_MODEL, IN_PROJ_WIDTH), D_MODEL ** -0.5),
        "conv_w": nrm(ks[3], (DEPTH, CONV_WIDTH, XBC_WIDTH), CONV_WIDTH ** -0.5),
        "conv_b": nrm(ks[4], (DEPTH, XBC_WIDTH), 0.02),
        "dt_bias": dt0 + jnp.log(-jnp.expm1(-dt0)),
        "a_log": jnp.log(jax.random.uniform(ks[6], (DEPTH, N_SSM_HEADS), f32, 1.0, 16.0)),
        "d_skip": 1.0 + nrm(ks[7], (DEPTH, N_SSM_HEADS), 0.1),
        "ssm_norm_w": 1.0 + nrm(ks[8], (DEPTH, D_INNER), 0.02),
        "w_attn_branch": nrm(ks[9], (DEPTH, ATTN_OUT_WIDTH, D_MODEL), ATTN_OUT_WIDTH ** -0.5),
        "w_ssm_branch": nrm(ks[10], (DEPTH, D_INNER, D_MODEL), D_INNER ** -0.5),
        "w_out": nrm(ks[11], (DEPTH, D_MODEL, D_MODEL), D_MODEL ** -0.5),
        "norm2_w": 1.0 + nrm(ks[12], (DEPTH, D_MODEL), 0.02),
        "w_ffn_in": nrm(ks[13], (DEPTH, D_MODEL, 2 * D_FF), D_MODEL ** -0.5),
        "w_ffn_out": nrm(ks[14], (DEPTH, D_FF, D_MODEL), D_FF ** -0.5),
        "rel_bias": nrm(ks[15], (N_REL_BUCKETS, N_ATTN_HEADS), 0.5),
        "final_norm_w": 1.0 + nrm(ks[16], (D_MODEL,), 0.02),
    }

def first_block(x, norm1_w, w_in, conv_w, conv_b, dt_bias, a_log, d_skip, ssm_norm_w,
              w_attn_branch, w_ssm_branch, w_out, norm2_w, w_ffn_in, w_ffn_out,
              rel_bias, final_norm_w):
    attn_biases = [rel_bias_block(rel_bias[:, g * HEADS_PER_GROUP:(g + 1) * HEADS_PER_GROUP], dil, window // dil)
                   for g, (window, dil) in enumerate(DILATED_GROUPS)]
    h = x
    for layer in range(DEPTH):
        h = h + hybrid_mixer(rmsnorm(h, norm1_w[layer]), w_in[layer], conv_w[layer], conv_b[layer],
                             dt_bias[layer], a_log[layer], d_skip[layer], ssm_norm_w[layer],
                             w_attn_branch[layer], w_ssm_branch[layer], w_out[layer], attn_biases)
        h = h + swiglu(rmsnorm(h, norm2_w[layer]), w_ffn_in[layer], w_ffn_out[layer])
    return rmsnorm(h, final_norm_w)


DEPTH_2 = 2

GRID_W = 64
CTX_LEN = 256
Q_BLOCK = 128
D_FF_2 = 2816
N_MOD = 9
ROPE_BASE = 10000.0
NEG = -1e30
A_HEADS = 8
A_KV_HEADS = 2
A_WINDOW = 128
B_HEADS = 4
B_V_DIM = 2 * HEAD_DIM
C_HEADS = 8
C_Q_RANK = 768
C_KV_RANK = 256
C_NOPE = 64
C_ROPE = 32
C_V = 64
D_HEADS = 8
D_WIN_ROWS = 8
D_WIN_COLS = 16
N_EVEN = (DEPTH_2 + 1) // 2
N_ODD = DEPTH_2 // 2
AB_SPLITS = (A_HEADS * HEAD_DIM, B_HEADS * 2 * HEAD_DIM, A_KV_HEADS * HEAD_DIM, A_KV_HEADS * HEAD_DIM, B_HEADS * 2 * HEAD_DIM, B_HEADS * B_V_DIM)
AB_Q_WIDTH = AB_SPLITS[0] + AB_SPLITS[1]
AB_IN = sum(AB_SPLITS)
AB_OUT = A_HEADS * HEAD_DIM + B_HEADS * B_V_DIM
CD_SPLITS = (C_Q_RANK, D_HEADS * HEAD_DIM, C_KV_RANK + C_ROPE, D_HEADS * HEAD_DIM, D_HEADS * HEAD_DIM)
CD_Q_WIDTH = CD_SPLITS[0] + CD_SPLITS[1]
CD_IN = sum(CD_SPLITS)
CD_OUT = C_HEADS * C_V + D_HEADS * HEAD_DIM


def split_cols(t, sizes):
    cuts = [int(v) for v in np.cumsum(sizes)[:-1]]
    return jnp.split(t, cuts, axis=-1)

def rms_norm(x, gain=None):
    xf = x.astype(jnp.float32)
    y = xf * lax.rsqrt(jnp.mean(xf * xf, axis=-1, keepdims=True) + EPS)
    if gain is not None:
        y = y * gain.astype(jnp.float32)
    return y.astype(x.dtype)

def modulate(h, shift, scale):
    return h * (1.0 + scale) + shift

def swiglu_2(h, w_gate, w_up, w_down):
    return (jax.nn.silu(h @ w_gate) * (h @ w_up)) @ w_down

def axial_rope_tables(n, rot_dim):
    nf = rot_dim // 4
    inv = ROPE_BASE ** (-jnp.arange(nf, dtype=jnp.float32) / nf)
    t = jnp.arange(n)
    row = (t // GRID_W).astype(jnp.float32)
    col = (t % GRID_W).astype(jnp.float32)
    ang = jnp.concatenate([row[:, None] * inv, col[:, None] * inv], axis=-1)
    return jnp.cos(ang), jnp.sin(ang)

def apply_rope2d(x, cos, sin):
    nf = x.shape[-1] // 4
    xf = x.astype(jnp.float32).reshape(x.shape[:-1] + (2, 2, nf))
    x1, x2 = xf[..., 0, :], xf[..., 1, :]
    c = cos.reshape(cos.shape[0], 1, 2, nf)
    s = sin.reshape(sin.shape[0], 1, 2, nf)
    out = jnp.stack([x1 * c - x2 * s, x2 * c + x1 * s], axis=-2)
    return out.reshape(x.shape).astype(x.dtype)

def joint_softmax(scores, sink=None):
    m = scores[0].max(axis=-1, keepdims=True)
    for s in scores[1:]:
        m = jnp.maximum(m, s.max(axis=-1, keepdims=True))
    if sink is not None:
        m = jnp.maximum(m, sink)
    es = [jnp.exp(s - m) for s in scores]
    denom = es[0].sum(axis=-1, keepdims=True)
    for e in es[1:]:
        denom = denom + e.sum(axis=-1, keepdims=True)
    if sink is not None:
        denom = denom + jnp.exp(sink - m)
    return [e / denom for e in es]

def sweep_blocks(fn, q, block):
    B, S = q.shape[0], q.shape[1]
    nb = S // block
    qb = jnp.moveaxis(q.reshape((B, nb, block) + q.shape[2:]), 1, 0)
    out = lax.map(lambda a: fn(a[0], a[1]), (qb, jnp.arange(nb)))
    return jnp.moveaxis(out, 0, 1).reshape((B, S) + out.shape[3:])

def gqa_attend(q, keyvals, sink=None):
    B, Q, H, d = q.shape
    kvh = keyvals[0][0].shape[2]
    g = H // kvh
    qg = q.reshape(B, Q, kvh, g, d)
    scores = []
    for k, _, mask in keyvals:
        s = jnp.einsum('bqhgd,bkhd->bhgqk', qg, k).astype(jnp.float32) * (d ** -0.5)
        if mask is not None:
            s = jnp.where(mask, s, NEG)
        scores.append(s)
    sink_b = None if sink is None else sink.astype(jnp.float32).reshape(kvh, g, 1, 1)
    probs = joint_softmax(scores, sink_b)
    out = None
    for p, (_, v, _) in zip(probs, keyvals):
        o = jnp.einsum('bhgqk,bkhd->bqhgd', p.astype(v.dtype), v)
        out = o if out is None else out + o
    return out.reshape(B, Q, H, d)

def windowed_sink_attention(q, k, v, k_ctx, v_ctx, sink):
    S = q.shape[1]
    span = Q_BLOCK + 2 * A_WINDOW
    pad = ((0, 0), (A_WINDOW, A_WINDOW), (0, 0), (0, 0))
    k_pad = jnp.pad(k, pad)
    v_pad = jnp.pad(v, pad)

    def block(q_blk, n):
        start = n * Q_BLOCK
        k_blk = lax.dynamic_slice_in_dim(k_pad, start, span, axis=1)
        v_blk = lax.dynamic_slice_in_dim(v_pad, start, span, axis=1)
        q_pos = start + jnp.arange(Q_BLOCK)
        k_pos = start - A_WINDOW + jnp.arange(span)
        mask = ((jnp.abs(q_pos[:, None] - k_pos[None, :]) <= A_WINDOW)
                & (k_pos >= 0)[None, :] & (k_pos < S)[None, :])
        return gqa_attend(q_blk, [(k_blk, v_blk, mask), (k_ctx, v_ctx, None)], sink)

    return sweep_blocks(block, q, Q_BLOCK)

def diff_lambda(lq1, lk1, lq2, lk2, lam_init):
    f = jnp.float32
    return (jnp.exp(jnp.sum(lq1.astype(f) * lk1.astype(f)))
            - jnp.exp(jnp.sum(lq2.astype(f) * lk2.astype(f))) + lam_init)

def diff_qk(t, gain, rope):
    B, n, _ = t.shape
    t = rms_norm(t.reshape(B, n, 2 * B_HEADS, HEAD_DIM), gain)
    if rope is not None:
        t = apply_rope2d(t, *rope)
    return t.reshape(B, n, B_HEADS, 2, HEAD_DIM)

def diff_attend(q, k, v, lam):
    s = jnp.einsum('bqhmd,bkhmd->bhmqk', q, k).astype(jnp.float32) * (HEAD_DIM ** -0.5)
    p = jax.nn.softmax(s, axis=-1)
    w = p[:, :, 0] - lam * p[:, :, 1]
    return jnp.einsum('bhqk,bkhe->bqhe', w.astype(v.dtype), v)

def mla_queries(dq, q_a_norm, w_uq, qn_nope, qn_rope, rope):
    B, n, _ = dq.shape
    q = (rms_norm(dq, q_a_norm) @ w_uq).reshape(B, n, C_HEADS, C_NOPE + C_ROPE)
    q_nope = rms_norm(q[..., :C_NOPE], qn_nope)
    q_rope = rms_norm(q[..., C_NOPE:], qn_rope)
    if rope is not None:
        q_rope = apply_rope2d(q_rope, *rope)
    return jnp.concatenate([q_nope, q_rope], axis=-1)

def mla_keys_values(dkv, kv_a_norm, w_ukv, kn_nope, kn_rope, rope):
    B, n, _ = dkv.shape
    c_kv, k_rope = dkv[..., :C_KV_RANK], dkv[..., C_KV_RANK:]
    kv = (rms_norm(c_kv, kv_a_norm) @ w_ukv).reshape(B, n, C_HEADS, C_NOPE + C_V)
    k_nope = rms_norm(kv[..., :C_NOPE], kn_nope)
    k_rope = rms_norm(k_rope, kn_rope)[:, :, None, :]
    if rope is not None:
        k_rope = apply_rope2d(k_rope, *rope)
    return k_nope, k_rope[:, :, 0, :], kv[..., C_NOPE:]

def mla_attend(q, k_nope, k_rope, v):
    q_nope, q_rope = q[..., :C_NOPE], q[..., C_NOPE:]
    s = (jnp.einsum('bqhd,bkhd->bhqk', q_nope, k_nope)
         + jnp.einsum('bqhr,bkr->bhqk', q_rope, k_rope)).astype(jnp.float32) * ((C_NOPE + C_ROPE) ** -0.5)
    p = jax.nn.softmax(s, axis=-1)
    return jnp.einsum('bhqk,bkhd->bqhd', p.astype(v.dtype), v)

def neighbourhood_attention(q, k, v, k_ctx, v_ctx, rpb):
    B, S, H, d = q.shape
    rows = S // GRID_W
    kh = min(D_WIN_ROWS, rows)
    kw = D_WIN_COLS
    k_grid = k.reshape(B, rows, GRID_W, H, d)
    v_grid = v.reshape(B, rows, GRID_W, H, d)
    cols = jnp.arange(GRID_W)
    col_start = jnp.clip(cols - kw // 2, 0, GRID_W - kw)
    col_mask = (cols[None, :] >= col_start[:, None]) & (cols[None, :] < col_start[:, None] + kw)
    dc_idx = jnp.clip(cols[None, :] - cols[:, None], -(kw - 1), kw - 1) + (D_WIN_COLS - 1)
    scale = d ** -0.5
    rpb_f = rpb.astype(jnp.float32)

    def row_block(q_row, r):
        row_start = jnp.clip(r - kh // 2, 0, rows - kh)
        k_band = lax.dynamic_slice_in_dim(k_grid, row_start, kh, axis=1)
        v_band = lax.dynamic_slice_in_dim(v_grid, row_start, kh, axis=1)
        dr_idx = row_start + jnp.arange(kh) - r + (D_WIN_ROWS - 1)
        bias = rpb_f[:, dr_idx[None, :, None], dc_idx[:, None, :]]
        s = jnp.einsum('bqhd,bjkhd->bhqjk', q_row, k_band).astype(jnp.float32) * scale + bias
        s = jnp.where(col_mask[:, None, :], s, NEG).reshape(B, H, GRID_W, kh * GRID_W)
        s_ctx = jnp.einsum('bqhd,bchd->bhqc', q_row, k_ctx).astype(jnp.float32) * scale
        p, p_ctx = joint_softmax([s, s_ctx])
        p = p.reshape(B, H, GRID_W, kh, GRID_W).astype(v.dtype)
        return (jnp.einsum('bhqjk,bjkhd->bqhd', p, v_band)
                + jnp.einsum('bhqc,bchd->bqhd', p_ctx.astype(v.dtype), v_ctx))

    return sweep_blocks(row_block, q, GRID_W)

def mix_window_diff(h, hc, w_in, w_out, a_q_norm, a_k_norm, a_sink, b_q_norm, b_k_norm,
                    b_lq1, b_lk1, b_lq2, b_lk2, b_sub_norm, lam_init, rope, need_ctx):
    B, S, _ = h.shape
    L = hc.shape[1]
    aq, bq, ak, av, bk, bv = split_cols(h @ w_in, AB_SPLITS)
    ak_c, av_c, bk_c, bv_c = split_cols(hc @ w_in[:, AB_Q_WIDTH:], AB_SPLITS[2:])
    aq = apply_rope2d(rms_norm(aq.reshape(B, S, A_HEADS, HEAD_DIM), a_q_norm), *rope)
    ak = apply_rope2d(rms_norm(ak.reshape(B, S, A_KV_HEADS, HEAD_DIM), a_k_norm), *rope)
    av = av.reshape(B, S, A_KV_HEADS, HEAD_DIM)
    ak_c = rms_norm(ak_c.reshape(B, L, A_KV_HEADS, HEAD_DIM), a_k_norm)
    av_c = av_c.reshape(B, L, A_KV_HEADS, HEAD_DIM)
    y_a = windowed_sink_attention(aq, ak, av, ak_c, av_c, a_sink)
    lam = diff_lambda(b_lq1, b_lk1, b_lq2, b_lk2, lam_init)
    bq = diff_qk(bq, b_q_norm, rope)
    bk = diff_qk(bk, b_k_norm, rope)
    bv = bv.reshape(B, S, B_HEADS, B_V_DIM)
    bk_c = diff_qk(bk_c, b_k_norm, None)
    bv_c = bv_c.reshape(B, L, B_HEADS, B_V_DIM)
    k_all = jnp.concatenate([bk_c, bk], axis=1)
    v_all = jnp.concatenate([bv_c, bv], axis=1)
    y_b = sweep_blocks(lambda q_blk, n: diff_attend(q_blk, k_all, v_all, lam), bq, Q_BLOCK)
    y_b = rms_norm(y_b, b_sub_norm) * (1.0 - lam_init)
    y = jnp.concatenate([y_a.reshape(B, S, -1), y_b.reshape(B, S, -1)], axis=-1) @ w_out
    if not need_ctx:
        return y, None
    aq_c, bq_c = split_cols(hc @ w_in[:, :AB_Q_WIDTH], AB_SPLITS[:2])
    aq_c = rms_norm(aq_c.reshape(B, L, A_HEADS, HEAD_DIM), a_q_norm)
    y_a_c = gqa_attend(aq_c, [(ak_c, av_c, None)], a_sink)
    y_b_c = rms_norm(diff_attend(diff_qk(bq_c, b_q_norm, None), bk_c, bv_c, lam), b_sub_norm) * (1.0 - lam_init)
    y_c = jnp.concatenate([y_a_c.reshape(B, L, -1), y_b_c.reshape(B, L, -1)], axis=-1) @ w_out
    return y, y_c

def mix_mla_neighbourhood(h, hc, w_in, w_out, c_q_a_norm, c_kv_a_norm, c_w_uq, c_w_ukv,
                          c_q_nope_norm, c_q_rope_norm, c_k_nope_norm, c_k_rope_norm,
                          d_q_norm, d_k_norm, d_rpb, rope, need_ctx):
    B, S, _ = h.shape
    L = hc.shape[1]
    cq, dq, ckv, dk, dv = split_cols(h @ w_in, CD_SPLITS)
    ckv_c, dk_c, dv_c = split_cols(hc @ w_in[:, CD_Q_WIDTH:], CD_SPLITS[2:])
    q = mla_queries(cq, c_q_a_norm, c_w_uq, c_q_nope_norm, c_q_rope_norm, rope)
    kn, kr, v = mla_keys_values(ckv, c_kv_a_norm, c_w_ukv, c_k_nope_norm, c_k_rope_norm, rope)
    kn_c, kr_c, v_c = mla_keys_values(ckv_c, c_kv_a_norm, c_w_ukv, c_k_nope_norm, c_k_rope_norm, None)
    kn_all = jnp.concatenate([kn_c, kn], axis=1)
    kr_all = jnp.concatenate([kr_c, kr], axis=1)
    v_all = jnp.concatenate([v_c, v], axis=1)
    y_mla = sweep_blocks(lambda q_blk, n: mla_attend(q_blk, kn_all, kr_all, v_all), q, Q_BLOCK)
    dq = rms_norm(dq.reshape(B, S, D_HEADS, HEAD_DIM), d_q_norm)
    dk = rms_norm(dk.reshape(B, S, D_HEADS, HEAD_DIM), d_k_norm)
    dv = dv.reshape(B, S, D_HEADS, HEAD_DIM)
    dk_c = rms_norm(dk_c.reshape(B, L, D_HEADS, HEAD_DIM), d_k_norm)
    dv_c = dv_c.reshape(B, L, D_HEADS, HEAD_DIM)
    y_nat = neighbourhood_attention(dq, dk, dv, dk_c, dv_c, d_rpb)
    y = jnp.concatenate([y_mla.reshape(B, S, -1), y_nat.reshape(B, S, -1)], axis=-1) @ w_out
    if not need_ctx:
        return y, None
    cq_c, dq_c = split_cols(hc @ w_in[:, :CD_Q_WIDTH], CD_SPLITS[:2])
    y_mla_c = mla_attend(mla_queries(cq_c, c_q_a_norm, c_w_uq, c_q_nope_norm, c_q_rope_norm, None), kn_c, kr_c, v_c)
    y_nat_c = gqa_attend(rms_norm(dq_c.reshape(B, L, D_HEADS, HEAD_DIM), d_q_norm), [(dk_c, dv_c, None)])
    y_c = jnp.concatenate([y_mla_c.reshape(B, L, -1), y_nat_c.reshape(B, L, -1)], axis=-1) @ w_out
    return y, y_c

def second_inputs(seed: int = 0) -> dict:
    key = jax.random.key(seed)
    ks = jax.random.split(key, 37)
    f32 = jnp.float32

    def nrm(i, shape, scale):
        return scale * jax.random.normal(ks[i], shape, f32)

    def gain(i, shape):
        return 1.0 + 0.05 * jax.random.normal(ks[i], shape, f32)

    D, F, NE, NO = D_MODEL, D_FF_2, N_EVEN, N_ODD
    return {
        "x": nrm(0, (BATCH, SEQ, D), 1.0),
        "c": nrm(1, (BATCH, D), 1.0),
        "ctx": nrm(2, (BATCH, CTX_LEN, D), 1.0),
        "c_ctx": nrm(3, (D,), 1.0),
        "w_mod": nrm(4, (DEPTH_2, D, N_MOD * D), 0.5 * D ** -0.5),
        "b_mod": nrm(5, (DEPTH_2, N_MOD * D), 0.02),
        "ffn1_w_gate": nrm(6, (DEPTH_2, D, F), D ** -0.5),
        "ffn1_w_up": nrm(7, (DEPTH_2, D, F), D ** -0.5),
        "ffn1_w_down": nrm(8, (DEPTH_2, F, D), F ** -0.5),
        "ffn2_w_gate": nrm(9, (DEPTH_2, D, F), D ** -0.5),
        "ffn2_w_up": nrm(10, (DEPTH_2, D, F), D ** -0.5),
        "ffn2_w_down": nrm(11, (DEPTH_2, F, D), F ** -0.5),
        "ab_w_in": nrm(12, (NE, D, AB_IN), D ** -0.5),
        "ab_w_out": nrm(13, (NE, AB_OUT, D), AB_OUT ** -0.5),
        "a_q_norm": gain(14, (NE, HEAD_DIM)),
        "a_k_norm": gain(15, (NE, HEAD_DIM)),
        "a_sink": nrm(16, (NE, A_HEADS), 0.5),
        "b_q_norm": gain(17, (NE, HEAD_DIM)),
        "b_k_norm": gain(18, (NE, HEAD_DIM)),
        "b_lambda_q1": nrm(19, (NE, HEAD_DIM), 0.1),
        "b_lambda_k1": nrm(20, (NE, HEAD_DIM), 0.1),
        "b_lambda_q2": nrm(21, (NE, HEAD_DIM), 0.1),
        "b_lambda_k2": nrm(22, (NE, HEAD_DIM), 0.1),
        "b_sub_norm": gain(23, (NE, B_V_DIM)),
        "cd_w_in": nrm(24, (NO, D, CD_IN), D ** -0.5),
        "cd_w_out": nrm(25, (NO, CD_OUT, D), CD_OUT ** -0.5),
        "c_q_a_norm": gain(26, (NO, C_Q_RANK)),
        "c_kv_a_norm": gain(27, (NO, C_KV_RANK)),
        "c_w_uq": nrm(28, (NO, C_Q_RANK, C_HEADS * (C_NOPE + C_ROPE)), C_Q_RANK ** -0.5),
        "c_w_ukv": nrm(29, (NO, C_KV_RANK, C_HEADS * (C_NOPE + C_V)), C_KV_RANK ** -0.5),
        "c_q_nope_norm": gain(30, (NO, C_NOPE)),
        "c_q_rope_norm": gain(31, (NO, C_ROPE)),
        "c_k_nope_norm": gain(32, (NO, C_NOPE)),
        "c_k_rope_norm": gain(33, (NO, C_ROPE)),
        "d_q_norm": gain(34, (NO, HEAD_DIM)),
        "d_k_norm": gain(35, (NO, HEAD_DIM)),
        "d_rpb": nrm(36, (NO, D_HEADS, 2 * D_WIN_ROWS - 1, 2 * D_WIN_COLS - 1), 0.5),
    }

def second_block(x, c, ctx, c_ctx, w_mod, b_mod,
              ffn1_w_gate, ffn1_w_up, ffn1_w_down, ffn2_w_gate, ffn2_w_up, ffn2_w_down,
              ab_w_in, ab_w_out, a_q_norm, a_k_norm, a_sink, b_q_norm, b_k_norm,
              b_lambda_q1, b_lambda_k1, b_lambda_q2, b_lambda_k2, b_sub_norm,
              cd_w_in, cd_w_out, c_q_a_norm, c_kv_a_norm, c_w_uq, c_w_ukv,
              c_q_nope_norm, c_q_rope_norm, c_k_nope_norm, c_k_rope_norm,
              d_q_norm, d_k_norm, d_rpb):
    S = x.shape[1]
    rope_head = axial_rope_tables(S, HEAD_DIM)
    rope_mla = axial_rope_tables(S, C_ROPE)
    c_act = jax.nn.silu(c)
    c_ctx_act = jax.nn.silu(c_ctx)
    xc = ctx
    for l in range(DEPTH_2):
        need_ctx = l < DEPTH_2 - 1
        mx = jnp.split((c_act @ w_mod[l] + b_mod[l])[:, None, :], N_MOD, axis=-1)
        mc = jnp.split((c_ctx_act @ w_mod[l] + b_mod[l])[None, None, :], N_MOD, axis=-1)
        ffn1 = (ffn1_w_gate[l], ffn1_w_up[l], ffn1_w_down[l])
        ffn2 = (ffn2_w_gate[l], ffn2_w_up[l], ffn2_w_down[l])
        x = x + 0.5 * mx[2] * swiglu_2(modulate(rms_norm(x), mx[0], mx[1]), *ffn1)
        xc = xc + 0.5 * mc[2] * swiglu_2(modulate(rms_norm(xc), mc[0], mc[1]), *ffn1)
        h = modulate(rms_norm(x), mx[3], mx[4])
        hc = modulate(rms_norm(xc), mc[3], mc[4])
        i = l // 2
        if l % 2 == 0:
            lam_init = 0.8 - 0.6 * math.exp(-0.3 * l)
            y, y_c = mix_window_diff(h, hc, ab_w_in[i], ab_w_out[i], a_q_norm[i], a_k_norm[i], a_sink[i],
                                     b_q_norm[i], b_k_norm[i], b_lambda_q1[i], b_lambda_k1[i],
                                     b_lambda_q2[i], b_lambda_k2[i], b_sub_norm[i], lam_init,
                                     rope_head, need_ctx)
        else:
            y, y_c = mix_mla_neighbourhood(h, hc, cd_w_in[i], cd_w_out[i], c_q_a_norm[i], c_kv_a_norm[i],
                                           c_w_uq[i], c_w_ukv[i], c_q_nope_norm[i], c_q_rope_norm[i],
                                           c_k_nope_norm[i], c_k_rope_norm[i], d_q_norm[i], d_k_norm[i],
                                           d_rpb[i], rope_mla, need_ctx)
        x = x + mx[5] * y
        x = x + 0.5 * mx[8] * swiglu_2(modulate(rms_norm(x), mx[6], mx[7]), *ffn2)
        if need_ctx:
            xc = xc + mc[5] * y_c
            xc = xc + 0.5 * mc[8] * swiglu_2(modulate(rms_norm(xc), mc[6], mc[7]), *ffn2)
    return x


def setup_inputs(seed=0):
    out = dict(first_inputs(seed))
    for name, value in second_inputs(seed + 1).items():
        if name != "x":
            out[name + "_2"] = value
    return out


def reference(
    x, norm1_w, w_in, conv_w, conv_b, dt_bias, a_log, d_skip, ssm_norm_w, w_attn_branch,
    w_ssm_branch, w_out, norm2_w, w_ffn_in, w_ffn_out, rel_bias, final_norm_w, c_2, ctx_2,
    c_ctx_2, w_mod_2, b_mod_2, ffn1_w_gate_2, ffn1_w_up_2, ffn1_w_down_2, ffn2_w_gate_2,
    ffn2_w_up_2, ffn2_w_down_2, ab_w_in_2, ab_w_out_2, a_q_norm_2, a_k_norm_2, a_sink_2,
    b_q_norm_2, b_k_norm_2, b_lambda_q1_2, b_lambda_k1_2, b_lambda_q2_2, b_lambda_k2_2,
    b_sub_norm_2, cd_w_in_2, cd_w_out_2, c_q_a_norm_2, c_kv_a_norm_2, c_w_uq_2, c_w_ukv_2,
    c_q_nope_norm_2, c_q_rope_norm_2, c_k_nope_norm_2, c_k_rope_norm_2, d_q_norm_2, d_k_norm_2,
    d_rpb_2,
):
    x = first_block(
        x, norm1_w, w_in, conv_w, conv_b, dt_bias, a_log, d_skip, ssm_norm_w, w_attn_branch,
        w_ssm_branch, w_out, norm2_w, w_ffn_in, w_ffn_out, rel_bias, final_norm_w,
    )
    return second_block(
        x, c_2, ctx_2, c_ctx_2, w_mod_2, b_mod_2, ffn1_w_gate_2, ffn1_w_up_2, ffn1_w_down_2,
        ffn2_w_gate_2, ffn2_w_up_2, ffn2_w_down_2, ab_w_in_2, ab_w_out_2, a_q_norm_2,
        a_k_norm_2, a_sink_2, b_q_norm_2, b_k_norm_2, b_lambda_q1_2, b_lambda_k1_2,
        b_lambda_q2_2, b_lambda_k2_2, b_sub_norm_2, cd_w_in_2, cd_w_out_2, c_q_a_norm_2,
        c_kv_a_norm_2, c_w_uq_2, c_w_ukv_2, c_q_nope_norm_2, c_q_rope_norm_2, c_k_nope_norm_2,
        c_k_rope_norm_2, d_q_norm_2, d_k_norm_2, d_rpb_2,
    )


_drawn_inputs = setup_inputs


def setup_inputs(seed=0):
    import zlib

    import numpy as np

    out = dict(_drawn_inputs(seed))
    spreads = {}
    factors = {'norm1_w': 3.155,
     'conv_b': 3.896,
     'ssm_norm_w': 5.359,
     'norm2_w': 4.305,
     'final_norm_w': 2.841,
     'a_q_norm_2': 8.0,
     'a_k_norm_2': 8.0,
     'a_sink_2': 8.0,
     'b_q_norm_2': 8.0,
     'b_k_norm_2': 8.0,
     'b_lambda_q1_2': 64.0,
     'b_lambda_k1_2': 64.0,
     'b_lambda_q2_2': 8.0,
     'b_lambda_k2_2': 8.0,
     'b_sub_norm_2': 6.444,
     'c_q_a_norm_2': 8.0,
     'c_kv_a_norm_2': 8.0,
     'c_w_uq_2': 3.077,
     'c_q_nope_norm_2': 8.0,
     'c_q_rope_norm_2': 8.0,
     'c_k_nope_norm_2': 8.0,
     'c_k_rope_norm_2': 8.0,
     'd_q_norm_2': 27.624,
     'd_k_norm_2': 30.631,
     'd_rpb_2': 41.036}
    for name, (base, spread) in spreads.items():
        noise = np.random.default_rng([zlib.crc32(name.encode()), seed]).standard_normal(out[name].shape)
        drawn = base * np.exp(spread * noise) if base else spread * noise
        out[name] = jnp.asarray(drawn.astype(out[name].dtype))
    for name, factor in factors.items():
        out[name] = (out[name] * factor).astype(out[name].dtype)
    return out
```

```python
from contextlib import ExitStack

import numpy as np

import concourse.bass as bass
from concourse import mybir

ALU = mybir.AluOpType
ACT = mybir.ActivationFunctionType
F32 = mybir.dt.float32
AX = mybir.AxisListType

P = 128
S = 256
NT = S // P
D = 1024
KD = D // P
HD = 64
EPS = 1e-6
NEG = -1e30

DILATIONS = (1, 4, 16)
WINDOWS = (128, 512, 2048)
NG = len(DILATIONS)
HG = 8
AW = NG * HG * HD
N_BUCKETS, REL_MAX = 32, 2048

DI = 2 * D
KI = DI // P
SH = DI // 64
SG = 4
SHG = SH // SG
GW = DI // SG
CONV = 4
XBC = DI + 2 * SG * 128
KX = XBC // P

FF = 2816
KF = FF // P
NMOD = 9
LAYERS = 2

CW = 256
RING = 4
SLOT = 11 * CW
CRED = RING

GRID_W, WIN_COLS, WIN_ROWS = 64, 16, 8
ROWS = S // GRID_W
RPB_R, RPB_C = 2 * WIN_ROWS - 1, 2 * WIN_COLS - 1
RPB_PAD = 2 * GRID_W - 1

QR, KVR, ROPE = 768, 256, 32
MQ = HD + ROPE

TOEP = 3 * P - 1



def bucket(dist):
    exact = N_BUCKETS // 2
    d = np.maximum(dist, 1).astype(np.float32)
    large = exact + (np.log(d / np.float32(exact)) / np.float32(np.log(REL_MAX / exact))
                     * np.float32(N_BUCKETS - exact)).astype(np.int32)
    return np.where(dist < exact, dist, np.minimum(large, N_BUCKETS - 1))


def rope_rows(width):
    nf = width // 4
    inv = (np.float32(10000.0) ** (-np.arange(nf, dtype=np.float32) / np.float32(nf))).astype(np.float32)
    t = np.arange(S)
    out_c, out_s = np.zeros((S, 2, 2, nf), np.float32), np.zeros((S, 2, 2, nf), np.float32)
    for axis, pos in enumerate((t // GRID_W, t % GRID_W)):
        ang = (pos.astype(np.float32)[:, None] * inv).astype(np.float32)
        out_c[:, axis] = np.cos(ang)[:, None]
        out_s[:, axis, 0], out_s[:, axis, 1] = -np.sin(ang), np.sin(ang)
    return out_c.reshape(S, width), out_s.reshape(S, width)


def by_tile(a):
    return a.reshape(NT, P, -1).transpose(1, 0, 2).reshape(P, -1)


def shape_constants():
    p = np.arange(P)
    i, j = np.arange(S)[:, None], np.arange(S)[None]
    c64, s64 = rope_rows(HD)
    c32, s32 = rope_rows(ROPE)
    upper = (p[:, None] <= p[None]).astype(np.float32)
    dist = TOEP - 1 - np.arange(TOEP) - (P - 1)
    onehot = np.zeros((P, TOEP), np.float32)
    onehot[bucket(np.maximum(dist, 0)), np.arange(TOEP)] = 1
    relmask = np.zeros((P, TOEP), np.float32)
    for g, (dil, win) in enumerate(zip(DILATIONS, WINDOWS)):
        ok = (dist >= 0) & (dist <= win) & (dist % dil == 0)
        relmask[g * HG:(g + 1) * HG] = np.where(ok, 0, NEG)
    col = np.arange(GRID_W)
    first = np.clip(col - WIN_COLS // 2, 0, GRID_W - WIN_COLS)
    inside = (col[None] >= first[:, None]) & (col[None] < first[:, None] + WIN_COLS)
    parts = {
        "ident": np.eye(P, dtype=np.float32),
        "mirror": np.eye(P, dtype=np.float32)[::-1],
        "mirror64": np.kron(np.eye(2, dtype=np.float32), np.eye(GRID_W, dtype=np.float32)[::-1]),
        "ones": np.ones((P, P), np.float32),
        "upper": np.concatenate([upper, np.ones((P, P), np.float32)], 1),
        "causal": np.concatenate([np.where(upper > 0, 0, NEG).astype(np.float32), np.zeros((P, P), np.float32)], 1),
        "window": by_tile(np.where(abs(i - j) <= 128, 0, NEG).astype(np.float32)),
        "colmask": np.tile(np.where(inside, 0, NEG).astype(np.float32), (2, ROWS)),
        "cos64": by_tile(c64), "sin64": by_tile(s64), "cos32": by_tile(c32), "sin32": by_tile(s32),
        "onehot": onehot, "relmask": relmask,
    }
    where, at = {}, 0
    for name, a in parts.items():
        where[name] = (at, a.shape[1])
        at += a.shape[1]
    return np.concatenate(list(parts.values()), 1).astype(np.float32), where


COLS = {}
for _name, _n in (("norm1", KD), ("norm2", KD), ("final", KD), ("conv_w", CONV * KX), ("conv_b", KX),
                  ("ssm_norm", KI), ("b_mod", LAYERS * NMOD * KD), ("cond", 2 * KD), ("b_sub", 1),
                  ("cq_norm", QR // P), ("ckv_norm", KVR // P)):
    COLS[_name] = (sum(n for _, n in COLS.values()), _n)
ROWV = {}
for _name, _n in (("dt_bias", SH), ("a_log", SH), ("d_skip", SH), ("aq", HD), ("ak", HD), ("bq", HD), ("bk", HD),
                  ("dq", HD), ("dk", HD), ("cqn", HD), ("cqr", ROPE), ("ckn", HD), ("ckr", ROPE), ("sink", 8),
                  ("lq1", HD), ("lk1", HD), ("lq2", HD), ("lk2", HD)):
    ROWV[_name] = (sum(n for _, n in ROWV.values()), _n)
N_COLS, N_ROWV = sum(n for _, n in COLS.values()), sum(n for _, n in ROWV.values())



class Steps:

    def __init__(self, engine, sem):
        self.engine, self.sem, self.done, self.loop = engine, sem, 0, 0

    def __call__(self, instruction):
        instruction.then_inc(self.sem, 1)
        self.done += 1
        self.engine.wait_ge(self.sem, self.loop + self.done)


class Chunk:

    def __init__(self, first, i, j):
        at = first + j
        self.index = RING * i + j
        self.slot = at % RING
        self.landed = 16 * RING // RING * i + 16 * (at // RING + 1)
        self.number = RING * i + at
        self.bank = 2 * self.slot
        self.j = j % RING


def each_chunk(engine, first, count, body, steps=None, per_chunk=0):
    loops = count // RING
    if loops < 2:
        loops = 0
    if loops:
        start = steps.done if steps else 0
        with engine.Fori(0, loops) as i:
            if steps:
                steps.loop = i * (int(RING * per_chunk))
            for j in range(RING):
                body(Chunk(first, i, j))
        if steps:
            assert steps.done == start + RING * per_chunk, (steps.done - start, int(RING * per_chunk))
            steps.loop, steps.done = 0, start + loops * int(RING * per_chunk)
    for j in range(loops * RING, count):
        body(Chunk(first, 0, j))


def pick(ap3, index):
    return ap3[:, bass.ds(index, 1), :].rearrange("p a n -> p (a n)")


def build(nc, W, consts, where, out, taps=None, stop_after=None):
    with ExitStack() as ctx:
        def sb(name, *free):
            return ctx.enter_context(nc.sbuf_tensor(name, [P, *free], F32))

        def sem(name):
            return ctx.enter_context(nc.semaphore(name))

        ring = sb("ring", RING, SLOT)
        resid = sb("resid", KD, 2 * S)
        normed = sb("normed", KD, 2 * S)
        const = sb("const", where["onehot"][0])
        cols = sb("cols", N_COLS)
        rowv = sb("rowv", N_ROWV)
        mod = sb("mod", LAYERS * NMOD * KD, 2)
        small = sb("small", 768)
        w_dt = sb("w_dt", KD, SH)
        w_kr = sb("w_kr", KD, ROPE)
        rstd = sb("rstd", 2 * S)
        hidden = sb("hidden", KF, 2 * S)
        arena = sb("arena", 16384)
        psum = ctx.enter_context(nc.psum_tensor("psum", [P, 8, 512], F32))
        work = hidden[:].rearrange("p k t -> p (k t)")

        def C(name):
            a, n = where[name]
            return const[:, a:a + n]

        def col(name, k=0, n=1):
            a = COLS[name][0] + k
            return cols[:, a:a + n]

        def row(name):
            a, n = ROWV[name]
            return rowv[:, a:a + n]

        ident = C("ident")
        ones = C("ones")

        landed = [sem(f"weights_landed_{s}") for s in range(RING)]
        chunk_done = sem("chunk_done")
        chunk_free = sem("chunk_free")
        stage_end = sem("stage_end")
        const_in = sem("constants_landed")
        bias_in = sem("bias_landed")
        bias_rows = sem("bias_rows_ready")
        act_step, dve_step = sem("act_step"), sem("dve_step")
        mm = sem("tensor_ready")
        av = sem("scalar_ready")
        vv = sem("vector_ready")
        out_done = sem("output_written")
        at_scores, at_read, at_max, at_exp, at_probs, at_turned, at_copied, at_pv, at_out = (
            sem("attn_" + n) for n in ("scores_ready", "scores_read", "max_ready", "exp_ready", "probs_ready",
                                       "probs_turned", "turned_copied", "values_ready", "values_read"))

        scan_sums, scan_read, scan_exp, scan_masked, scan_y, scan_gated = (
            sem("scan_" + n) for n in ("sums_ready", "sums_read", "exp_ready", "masked_ready", "y_ready", "y_read"))

        block = ctx.enter_context(nc.Block())
        te, ve, se, ge = nc.tensor, nc.vector, nc.scalar, nc.gpsimd

        counts = {"mm": 0, "av": 0, "vv": 0, "chunks": 0, "units": 0, "bias": 48}

        def take(name, n):
            counts[name] += n
            return counts[name] - n

        scratch_rel = nc.dram_tensor("scratch_rel", (NG * HG, TOEP), F32, kind="Internal").ap()
        scratch_rpb = nc.dram_tensor("scratch_rpb", (8 * RPB_R, RPB_PAD), F32, kind="Internal").ap()


        class Stage:
            def sync(self, sp): pass
            def tensor(self, pe): pass
            def scalar(self, act, step): pass
            def vector(self, dve, step): pass

        class Stream(Stage):
            def stream(self, weights, rows, count):
                self.weights, self.rows, self.count = weights, rows, count
                self.first = take("chunks", count)

            def sync(self, sp):
                def load(ch):
                    sp.wait_ge(chunk_done, ch.number + 1)
                    sp.dma_start(ring[:, ch.slot, 0:self.rows * CW],
                                 self.weights[bass.ds(ch.index, 1)].rearrange("a p n -> p (a n)")
                                 ).then_inc(landed[ch.slot], 16)
                each_chunk(sp, self.first, self.count, load)

            def begin(self, pe, ch):
                pe.wait_ge(landed[ch.slot], ch.landed)
                pe.wait_ge(chunk_free, ch.number + 1)

        class Setup(Stage):
            def sync(self, sp):
                kept = where["onehot"][0]
                sp.dma_start(const[:], consts[:, 0:kept]).then_inc(const_in, 16)
                sp.dma_start(work[:, 1024:1024 + 2 * TOEP], consts[:, kept:kept + 2 * TOEP]).then_inc(const_in, 16)
                sp.dma_start(cols[:], W["cols"]).then_inc(const_in, 16)
                sp.dma_start(rowv[:], bass.AP(W["rowv"].tensor, 0, [[0, P], [1, N_ROWV]])).then_inc(const_in, 16)
                sp.dma_start(w_dt[:], W["w_dt"]).then_inc(const_in, 16)
                sp.dma_start(w_kr[:], W["w_kr"]).then_inc(const_in, 16)
                sp.dma_start(resid[:, :, 0:S], W["x"]).then_inc(const_in, 16)
                sp.dma_start(resid[:, :, S:2 * S], W["ctx"]).then_inc(const_in, 16)
                sp.dma_start(small[0:N_BUCKETS, 0:NG * HG], W["rel_bias"]).then_inc(const_in, 16)
                sp.wait_ge(bias_rows, 1)
                sp.dma_start(work[0:8 * RPB_R, 512 + 48:512 + 48 + RPB_C], W["rpb"]).then_inc(bias_in, 16)
                sp.wait_ge(bias_in, 16)
                sp.dma_start(scratch_rpb, work[0:8 * RPB_R, 512:512 + RPB_PAD]).then_inc(bias_in, 16)
                sp.wait_ge(bias_rows, 2)
                sp.dma_start(scratch_rel, work[0:NG * HG, 0:TOEP]).then_inc(bias_in, 16)
                sp.wait_ge(bias_in, 48)

            def tensor(self, pe):
                pe.wait_ge(const_in, 9 * 16)
                te.matmul(psum[0:NG * HG, 0, 0:TOEP], small[0:N_BUCKETS, 0:NG * HG],
                          work[0:N_BUCKETS, 1024:1024 + TOEP], start=True, stop=True).then_inc(mm, 1)

            def scalar(self, act, step):
                act.wait_ge(const_in, 9 * 16)

            def vector(self, dve, step):
                ve.memset(small[:, 760:764], 0.0).then_inc(chunk_done, CRED)
                ve.memset(small[:, 764:768], 0.0).then_inc(chunk_free, CRED)
                ve.memset(work[:, 512:512 + RPB_PAD], 0.0).then_inc(bias_rows, 1)
                dve.wait_ge(const_in, 9 * 16)
                dve.wait_ge(mm, self.mm0 + 1)
                ve.tensor_tensor(work[0:NG * HG, 0:TOEP], psum[0:NG * HG, 0, 0:TOEP],
                                 work[0:NG * HG, 1024 + TOEP:1024 + 2 * TOEP], ALU.add).then_inc(bias_rows, 1)

            def __init__(self):
                self.mm0 = take("mm", 1)

        class Modulation(Stream):
            def __init__(self, layer):
                self.layer, self.n = layer, NMOD * D // CW
                self.stream(W["w_mod"][layer * self.n:(layer + 1) * self.n], KD, self.n)
                self.cond = small[:, 32:32 + 2 * KD]
                self.tmp = small[:, 64:64 + 2 * KD]
                self.rows_sb = work[0:2, 0:self.n * CW]
                self.mm0, self.vv0, self.av0 = take("mm", 1), take("vv", 1), take("av", 1)

            def tensor(self, pe):
                pe.wait_ge(vv, self.vv0 + 1)
                cond = self.cond.rearrange("p (k c) -> p k c", c=2)

                def body(ch):
                    self.begin(pe, ch)
                    for k in range(KD):
                        last = te.matmul(psum[0:2, ch.bank, 0:CW], cond[:, k, :],
                                         ring[:, ch.slot, k * CW:(k + 1) * CW], start=(k == 0), stop=(k == KD - 1))
                    last.then_inc(chunk_done, 1)
                each_chunk(pe, self.first, self.count, body)
                pe.wait_ge(chunk_free, CRED + self.first + self.count)
                for m in range(NMOD * KD):
                    last = te.matmul(psum[:, 0, 2 * m:2 * m + 2], self.rows_sb[:, m * P:(m + 1) * P],
                                     ident[0:2, 0:2], start=True, stop=True)
                last.then_inc(mm, 1)

            def scalar(self, act, step):
                se.activation(self.tmp, col("cond", 0, 2 * KD), ACT.Exp, scale=-1.0).then_inc(av, 1)

                def body(ch):
                    act.wait_ge(chunk_done, CRED + ch.number + 1)
                    se.copy(self.rows_sb[:, bass.ds(ch.index * CW, CW)], psum[0:2, ch.bank, 0:CW]).then_inc(chunk_free, 1)
                each_chunk(act, self.first, self.count, body)

            def vector(self, dve, step):
                dve.wait_ge(av, self.av0 + 1)
                step(ve.tensor_scalar(self.tmp, self.tmp, 1.0, None, ALU.add))
                step(ve.reciprocal(self.tmp, self.tmp))
                ve.tensor_tensor(self.cond, self.tmp, col("cond", 0, 2 * KD), ALU.mult).then_inc(vv, 1)
                dve.wait_ge(mm, self.mm0 + 1)
                nm = NMOD * KD
                mine = mod[:, self.layer * nm:(self.layer + 1) * nm, :]
                bm = col("b_mod", self.layer * nm, nm)
                for side in range(2):
                    last = ve.tensor_tensor(mine[:, :, side], psum[:, 0, side:2 * nm:2], bm, ALU.add)
                step(last)
                for which in (1, 4, 7):
                    a = mine[:, which * KD:(which + 1) * KD, :]
                    ve.tensor_scalar(a, a, 1.0, None, ALU.add)
                for which in (2, 8):
                    a = mine[:, which * KD:(which + 1) * KD, :]
                    ve.tensor_scalar(a, a, 0.5, None, ALU.mult)



        class LinearT(Stream):
            def __init__(self, weights, rows, count, x, tiles, dest):
                self.stream(weights, rows, count)
                self.x, self.tiles, self.dest = x, tiles, dest

            def tensor(self, pe):
                def body(ch):
                    self.begin(pe, ch)
                    for t in range(self.tiles):
                        for k in range(self.rows):
                            last = te.matmul(psum[:, ch.bank + t // 2, (t % 2) * CW:(t % 2 + 1) * CW],
                                             self.x[:, k, t * P:(t + 1) * P], ring[:, ch.slot, k * CW:(k + 1) * CW],
                                             start=(k == 0), stop=(k == self.rows - 1))
                    last.then_inc(chunk_done, 1)
                each_chunk(pe, self.first, self.count, body)

            def scalar(self, act, step):
                def body(ch):
                    act.wait_ge(chunk_done, CRED + ch.number + 1)
                    for b in range(self.tiles // 2):
                        last = se.copy(self.dest[:, 2 * b:2 * b + 2, bass.ds(ch.index * CW, CW)],
                                       psum[:, ch.bank + b, :].rearrange("p (t n) -> p t n", t=2))
                    last.then_inc(chunk_free, 1)
                each_chunk(act, self.first, self.count, body)

        class LinearF(Stream):
            def __init__(self, weights, rows, count, x, width, dest, into_resid=False, gate=None):
                self.stream(weights, rows, count)
                self.x, self.width, self.dest, self.into_resid, self.gate = x, width, dest, into_resid, gate

            def tensor(self, pe):
                def body(ch):
                    self.begin(pe, ch)
                    for m in range(2):
                        for k in range(self.rows):
                            last = te.matmul(psum[:, ch.bank + m, 0:self.width],
                                             ring[:, ch.slot, k * CW + m * P:k * CW + (m + 1) * P],
                                             self.x[:, k, 0:self.width], start=(k == 0), stop=(k == self.rows - 1))
                    last.then_inc(chunk_done, 1)
                each_chunk(pe, self.first, self.count, body)

            def scalar(self, act, step):
                def body(ch):
                    act.wait_ge(chunk_done, CRED + ch.number + 1)
                    se.copy(self.dest[:, bass.ds(2 * ch.index, 2), 0:self.width],
                            psum[:, ch.bank:ch.bank + 2, 0:self.width]).then_inc(chunk_free, 1)
                if not self.into_resid:
                    each_chunk(act, self.first, self.count, body)

            def vector(self, dve, step):
                def body(ch):
                    dve.wait_ge(chunk_done, CRED + ch.number + 1)
                    add_to_resid(2 * ch.index, ch.bank, self.width, self.gate).then_inc(chunk_free, 1)
                if self.into_resid:
                    each_chunk(dve, self.first, self.count, body)

        def add_to_resid(tile, bank, width, gate):
            if gate is None:
                r = resid[:, bass.ds(tile, 2), 0:width]
                return ve.tensor_tensor(r, r, psum[:, bank:bank + 2, 0:width], ALU.add)
            base = (gate[0] * NMOD + gate[1]) * KD
            for m in range(2):
                for side in range(width // S):
                    a = slice(side * S, (side + 1) * S)
                    r = pick(resid[:, :, a], tile + m)
                    last = ve.scalar_tensor_tensor(
                        out=r, in0=psum[:, bank + m, a], scalar=pick(mod[:, base:base + KD, side:side + 1], tile + m),
                        in1=r, op0=ALU.mult, op1=ALU.add)
            return last

        class Norm(Stage):
            def __init__(self, width, gain, shift, out):
                self.width, self.gain, self.shift, self.out = width, gain, shift, out
                self.mm0, self.vv0, self.av0 = take("mm", 1), take("vv", 1 + KD), take("av", KD + 1)
                self.squares = hidden[:, 0:KD, 0:width]

            def tensor(self, pe):
                for k in range(KD):
                    pe.wait_ge(av, self.av0 + k + 1)
                    last = te.matmul(psum[:, 0, 0:self.width], ones, self.squares[:, k, :],
                                     start=(k == 0), stop=(k == KD - 1))
                last.then_inc(mm, 1)

            def scalar(self, act, step):
                w = self.width
                for k in range(KD):
                    se.activation(self.squares[:, k, :], resid[:, k, 0:w], ACT.Square).then_inc(av, 1)
                act.wait_ge(vv, self.vv0 + 1)
                step(se.activation(rstd[:, 0:w], rstd[:, 0:w], ACT.Ln))
                se.activation(rstd[:, 0:w], rstd[:, 0:w], ACT.Exp, scale=-0.5).then_inc(av, 1)
                if self.shift is not None:
                    for k in range(KD):
                        act.wait_ge(vv, self.vv0 + 2 + k)
                        for side in range(w // S):
                            a = self.out[:, k, side * S:(side + 1) * S]
                            se.activation(a, a, ACT.Identity, bias=self.shift(k, side))

            def vector(self, dve, step):
                w = self.width
                dve.wait_ge(mm, self.mm0 + 1)
                ve.tensor_scalar(rstd[:, 0:w], psum[:, 0, 0:w], 1.0 / D, EPS, ALU.mult, ALU.add).then_inc(vv, 1)
                dve.wait_ge(av, self.av0 + KD + 1)
                for k in range(KD):
                    for side in range(w // S):
                        a = slice(side * S, (side + 1) * S)
                        last = ve.scalar_tensor_tensor(out=self.out[:, k, a], in0=resid[:, k, a],
                                                       scalar=self.gain(k, side), in1=rstd[:, a],
                                                       op0=ALU.mult, op1=ALU.mult)
                    last.then_inc(vv, 1)

        def modulated(layer, shift, scale, width):
            return Norm(width, lambda k, s: mod[:, (layer * NMOD + scale) * KD + k, s:s + 1],
                        lambda k, s: mod[:, (layer * NMOD + shift) * KD + k, s:s + 1], normed)

        class FfnUp(Stream):
            def __init__(self, weights, width):
                self.stream(weights, KD, 2 * KF // 2)
                self.width = width
                self.av0 = take("av", self.count)
                self.sig = arena[:, 0:2 * 2 * width].rearrange("p (b m t) -> p b m t", b=2, m=2)

            def tensor(self, pe):
                def body(ch):
                    self.begin(pe, ch)
                    for m in range(2):
                        for k in range(KD):
                            last = te.matmul(psum[:, ch.bank + m, 0:self.width],
                                             ring[:, ch.slot, k * CW + m * P:k * CW + (m + 1) * P],
                                             normed[:, k, 0:self.width], start=(k == 0), stop=(k == KD - 1))
                    last.then_inc(chunk_done, 1)
                each_chunk(pe, self.first, self.count, body)

            def scalar(self, act, step):
                def body(ch):
                    if ch.j % 2 == 0:
                        act.wait_ge(chunk_done, CRED + ch.number + 1)
                        act.wait_ge(chunk_free, ch.number + CRED - 2)
                        se.activation(self.sig[:, ch.j // 2], psum[:, ch.bank:ch.bank + 2, 0:self.width],
                                      ACT.Exp, scale=-1.0).then_inc(av, 2)
                each_chunk(act, self.first, self.count, body)

            def vector(self, dve, step):
                def body(ch):
                    if ch.j % 2 == 0:
                        self.gate_bank = ch.bank
                        return
                    sig = self.sig[:, ch.j // 2]
                    dve.wait_ge(av, self.av0 + ch.index + 1)
                    step(ve.tensor_scalar(sig, sig, 1.0, None, ALU.add))
                    step(ve.reciprocal(sig, sig))
                    step(ve.tensor_tensor(sig, sig, psum[:, self.gate_bank:self.gate_bank + 2, 0:self.width],
                                          ALU.mult))
                    dve.wait_ge(chunk_done, CRED + ch.number + 1)
                    ve.tensor_tensor(hidden[:, bass.ds(ch.index - 1, 2), 0:self.width], sig,
                                     psum[:, ch.bank:ch.bank + 2, 0:self.width], ALU.mult).then_inc(chunk_free, 2)
                each_chunk(dve, self.first, self.count, body, step, 1.5)

        class FfnDown(Stream):
            def __init__(self, weights, width, gate):
                self.stream(weights, KF // 2, 2 * D // CW)
                self.width, self.gate = width, gate

            def tensor(self, pe):
                def body(ch):
                    self.begin(pe, ch)
                    half = ch.j % 2
                    bank = 2 * ((ch.slot - half) % RING)
                    for m in range(2):
                        for k in range(KF // 2):
                            last = te.matmul(psum[:, bank + m, 0:self.width],
                                             ring[:, ch.slot, k * CW + m * P:k * CW + (m + 1) * P],
                                             hidden[:, half * (KF // 2) + k, 0:self.width],
                                             start=(half == 0 and k == 0), stop=(half == 1 and k == KF // 2 - 1))
                    last.then_inc(chunk_done, 1)
                each_chunk(pe, self.first, self.count, body)

            def vector(self, dve, step):
                def body(ch):
                    if ch.j % 2 == 1:
                        dve.wait_ge(chunk_done, CRED + ch.number + 1)
                        add_to_resid(ch.index - 1, 2 * ((ch.slot - 1) % RING), self.width,
                                     self.gate).then_inc(chunk_free, 2)
                each_chunk(dve, self.first, self.count, body)


        class Map:
            def __init__(self, scores, biases, sink=None):
                self.scores, self.biases, self.sink = scores, biases, sink
                self.width = sum(n for n, _ in biases)

        class Unit:
            def __init__(self, maps, values, out, scale, lam=None):
                self.maps, self.values, self.out, self.scale, self.lam = maps, values, out, scale, lam

        class Attention(Stage):
            def __init__(self, units, space):
                self.units = units
                self.base = take("units", len(units))
                w = max(max(sum(m.width for m in u.maps), 128) for u in units)
                self.s = space[:, 0:2 * w].rearrange("p (b n) -> p b n", b=2)
                tiles = max(len(u.values) for u in units)
                self.turned = space[:, 2 * w:2 * w + tiles * P]
                self.stat = small[:, 128:128 + 32].rearrange("p (b n) -> p b n", b=2)

            def tensor(self, pe):
                for u in range(len(self.units) + 1):
                    if u < len(self.units):
                        unit, b = self.units[u], self.base + u
                        if u >= 2:
                            pe.wait_ge(at_read, b - 1)
                        for n, m in enumerate(unit.maps):
                            at = 0
                            for q, keys in m.scores:
                                width = keys.shape[1]
                                bank, off = divmod((2 * (u % 2) + n) * 512 + at, 512)
                                last = te.matmul(psum[:, bank, off:off + width], q, keys, start=True, stop=True)
                                at += width
                        last.then_inc(at_scores, 1)
                    if u >= 1:
                        unit, b = self.units[u - 1], self.base + u - 1
                        pe.wait_ge(at_probs, b + 1)
                        probs = self.s[:, (u - 1) % 2, :]
                        for j in range(len(unit.values)):
                            last = te.transpose(psum[:, 4 + j // 4, (j % 4) * P:(j % 4 + 1) * P],
                                                probs[:, j * P:(j + 1) * P], ident)
                        last.then_inc(at_turned, 1)
                        pe.wait_ge(at_copied, b + 1)
                        if u - 1 >= 2:
                            pe.wait_ge(at_out, b - 1)
                        for j, v in enumerate(unit.values):
                            last = te.matmul(psum[0:v.shape[1], 6 + (u - 1) % 2, 0:P], v,
                                             self.turned[:, j * P:(j + 1) * P],
                                             start=(j == 0), stop=(j == len(unit.values) - 1))
                        last.then_inc(at_pv, 1)

            def scalar(self, act, step):
                for u in range(len(self.units) + 1):
                    if u < len(self.units):
                        unit, b = self.units[u], self.base + u
                        act.wait_ge(at_max, b + 1)
                        at, stat = 0, self.stat[:, u % 2, :]
                        for n, m in enumerate(unit.maps):
                            a = self.s[:, u % 2, at:at + m.width]
                            last = se.activation(a, a, ACT.Exp, bias=stat[:, n:n + 1], accum_out=stat[:, 4 + n:5 + n])
                            if m.sink is not None:
                                last = se.activation(stat[:, 8 + n:9 + n], m.sink, ACT.Exp, bias=stat[:, n:n + 1])
                            at += m.width
                        last.then_inc(at_exp, 1)
                    if u >= 1:
                        unit, b = self.units[u - 1], self.base + u - 1
                        act.wait_ge(at_turned, b + 1)
                        n = len(unit.values) * P
                        se.copy(self.turned[:, 0:n], psum[:, 4:6, :].rearrange("p b n -> p (b n)")[:, 0:n]
                                ).then_inc(at_copied, 1)

            def vector(self, dve, step):
                flat = psum[:].rearrange("p b n -> p (b n)")
                for u in range(len(self.units) + 2):
                    if u >= 2:
                        unit, b = self.units[u - 2], self.base + u - 2
                        dve.wait_ge(at_pv, b + 1)
                        ve.tensor_copy(unit.out, psum[0:unit.out.shape[0], 6 + u % 2, 0:P]).then_inc(at_out, 1)
                    if u < len(self.units):
                        unit, b = self.units[u], self.base + u
                        dve.wait_ge(at_scores, b + 1)
                        at, stat = 0, self.stat[:, u % 2, :]
                        for n, m in enumerate(unit.maps):
                            inner = 0
                            for width, bias in m.biases:
                                off = (2 * (u % 2) + n) * 512 + inner
                                src, dst = flat[:, off:off + width], self.s[:, u % 2, at:at + width]
                                if bias is not None and len(bias.shape) == 3:
                                    src, dst = (a.rearrange("p (g n) -> p g n", g=bias.shape[1]) for a in (src, dst))
                                if bias is None:
                                    last = ve.tensor_scalar(dst, src, unit.scale, None, ALU.mult)
                                else:
                                    last = ve.scalar_tensor_tensor(out=dst, in0=src, scalar=unit.scale, in1=bias,
                                                                   op0=ALU.mult, op1=ALU.add)
                                at, inner = at + width, inner + width
                        last.then_inc(at_read, 1)
                        dve.wait_ge(at_read, b + 1)
                        at = 0
                        for n, m in enumerate(unit.maps):
                            last = ve.tensor_reduce(stat[:, n:n + 1], self.s[:, u % 2, at:at + m.width], AX.X, ALU.max,
                                                    negate=True)
                            at += m.width
                            if m.sink is not None:
                                step(last)
                                last = ve.scalar_tensor_tensor(out=stat[:, n:n + 1], in0=m.sink, scalar=-1.0,
                                                               in1=stat[:, n:n + 1], op0=ALU.mult, op1=ALU.min)
                        last.then_inc(at_max, 1)
                    if 1 <= u <= len(self.units):
                        unit, b = self.units[u - 1], self.base + u - 1
                        dve.wait_ge(at_exp, b + 1)
                        stat, s = self.stat[:, (u - 1) % 2, :], self.s[:, (u - 1) % 2, :]
                        k = len(unit.maps)
                        if unit.maps[0].sink is not None:
                            step(ve.tensor_tensor(stat[:, 4:5], stat[:, 4:5], stat[:, 8:9], ALU.add))
                        step(ve.reciprocal(stat[:, 4:4 + k], stat[:, 4:4 + k]))
                        w = unit.maps[0].width
                        if k == 1:
                            last = ve.tensor_scalar(s[:, 0:w], s[:, 0:w], stat[:, 4:5], None, ALU.mult)
                        else:
                            step(ve.tensor_tensor(stat[:, 5:6], stat[:, 5:6], unit.lam, ALU.mult))
                            step(ve.tensor_scalar(s[:, w:2 * w], s[:, w:2 * w], stat[:, 5:6], None, ALU.mult))
                            last = ve.scalar_tensor_tensor(out=s[:, 0:w], in0=s[:, 0:w], scalar=stat[:, 4:5],
                                                           in1=s[:, w:2 * w], op0=ALU.mult, op1=ALU.subtract)
                        last.then_inc(at_probs, 1)


        qk1 = arena[:, 0:24 * S].rearrange("p (m t) -> p m t", t=S)
        v1 = arena[:, 24 * S:24 * S + NT * AW].rearrange("p (t n) -> p t n", t=NT)
        attn1 = arena[:, 15360:15360 + 4 * S].rearrange("p (m t) -> p m t", t=S)
        relbias = work[:, 4096:4096 + NG * HG * 2 * P].rearrange("p (h s j) -> p h s j", s=2, j=P)

        class Mirror(Stage):
            def __init__(self, flat, mirror, loads, mask=None):
                self.flat, self.mirror, self.loads, self.mask = flat, mirror, loads, mask
                self.n = flat.shape[1] // 512
                self.mm0, self.vv0 = take("mm", self.n), take("vv", self.n)
                self.landed = take("bias", 16 * len(loads)) + 16 * len(loads)

            def sync(self, sp):
                sp.wait_ge(stage_end, 3 * stages.index(self))
                for dst, src in self.loads:
                    sp.dma_start(dst, src).then_inc(bias_in, 16)

            def tensor(self, pe):
                pe.wait_ge(bias_in, self.landed)
                for b in range(self.n):
                    if b >= 8:
                        pe.wait_ge(vv, self.vv0 + b - 7)
                    te.matmul(psum[:, b % 8, :], self.mirror, self.flat[:, b * 512:(b + 1) * 512],
                              start=True, stop=True).then_inc(mm, 1)

            def vector(self, dve, step):
                for b in range(self.n):
                    dve.wait_ge(mm, self.mm0 + b + 1)
                    dst = self.flat[:, b * 512:(b + 1) * 512]
                    if self.mask is None:
                        ve.tensor_copy(dst, psum[:, b % 8, :]).then_inc(vv, 1)
                    else:
                        dst, src = (a.rearrange("p (r n) -> p r n", n=S) for a in (dst, psum[:, b % 8, :]))
                        ve.tensor_tensor(dst, src, self.mask.rearrange("p (o n) -> p o n", o=1).to_broadcast(
                            [P, 512 // S, S]), ALU.add).then_inc(vv, 1)

        def relative_bias():
            loads = [(relbias[:, :, s, :], bass.AP(scratch_rel.tensor, P * s, [[1, P], [TOEP, NG * HG], [1, P]]))
                     for s in range(2)]
            return Mirror(relbias.rearrange("p h s j -> p (h s j)"), C("mirror"), loads)

        def attention1_units():
            units = []
            for t in range(NT):
                for h in range(HG):
                    a = slice((h % 2) * HD, (h % 2 + 1) * HD)
                    scores, values = [], []
                    for g in range(NG):
                        tile = g * 4 + h // 2
                        scores.append((qk1[a, tile, t * P:(t + 1) * P], qk1[a, 12 + tile, 0:(t + 1) * P]))
                        values += [v1[:, kt, (g * HG + h) * HD:(g * HG + h + 1) * HD] for kt in range(t + 1)]
                    bias = relbias[:, h::HG, 1 - t:2, :].rearrange("p g s j -> p g (s j)")
                    units.append(Unit([Map(scores, [(NG * (t + 1) * P, bias)])], values,
                                      attn1[a, h // 2, t * P:(t + 1) * P], HD ** -0.5))
            return units

        xbc = arena[:, 0:KX * (S + CONV - 1)].rearrange("p (m t) -> p m t", t=S + CONV - 1)
        z1 = arena[:, 6216:6216 + NT * DI].rearrange("p (t n) -> p t n", t=NT)
        gates1 = arena[:, 10312:10312 + 2 * KD * S].rearrange("p (m t) -> p m t", t=S)
        conv = work[:, 0:KX * S].rearrange("p (m t) -> p m t", t=S)
        x_tok = arena[:, 0:NT * DI].rearrange("p (t n) -> p t n", t=NT)
        y_tok = work[:, 0:NT * DI].rearrange("p (t n) -> p t n", t=NT)
        xdt = work[:, 6144:6144 + NT * DI].rearrange("p (t n) -> p t n", t=NT)
        ssm_t = work[:, 6144:6144 + KI * S].rearrange("p (m t) -> p m t", t=S)
        decay = work[:, 10240:10240 + 768].rearrange("p (b n) -> p b n", b=2)
        spare = normed[:].rearrange("p k t -> p (k t)")
        cb = spare[:, 0:SG * 384].rearrange("p (g n) -> p g n", g=SG)
        merged2 = work[:, 0:KD * S].rearrange("p (m t) -> p m t", t=S)
        dt = small[:, 256:256 + NT * SH]
        neg_la = small[:, 320:320 + NT * SH]
        dta = small[:, 384:384 + NT * SH]
        a_exp = small[:, 448:448 + SH]
        ssq = small[:, 480:480 + NT * SG]
        dt_tmp = small[:, 512:512 + NT * SH]

        class Only(Stage):
            def __init__(self, engine, program):
                setter = {"tensor": 0, "scalar": 1, "vector": 2}[engine]
                self.which, self.program = setter, program

            def tensor(self, pe):
                if self.which == 0:
                    self.program()

            def scalar(self, act, step):
                if self.which == 1:
                    self.program(step)

            def vector(self, dve, step):
                if self.which == 2:
                    self.program(step)

        class ConvX(LinearF):
            def __init__(self):
                super().__init__(W["w_x"], KD, KX // 2, normed, S, xbc[:, :, CONV - 1:])
                self.vv0 = take("vv", 1)

            def scalar(self, act, step):
                act.wait_ge(vv, self.vv0 + 1)
                super().scalar(act, step)

            def vector(self, dve, step):
                ve.memset(xbc[:, :, 0:CONV - 1], 0.0).then_inc(vv, 1)
                dve.wait_ge(vv, self.vv0 + 1)
                conv_w = [col("conv_w", w * KX, KX).rearrange("p (k o) -> p k o", o=1) for w in range(CONV)]
                conv_b = col("conv_b", 0, KX).rearrange("p (k o) -> p k o", o=1)

                def body(ch):
                    dve.wait_ge(chunk_free, CRED + ch.number + 1)
                    for m in range(2):
                        tile = 2 * ch.index + m
                        y = pick(conv, tile)
                        for w in range(CONV):
                            x_w = pick(xbc[:, :, w:w + S], tile)
                            if w == 0:
                                step(ve.tensor_scalar(y, x_w, pick(conv_w[0], tile), pick(conv_b, tile),
                                                      ALU.mult, ALU.add))
                            else:
                                step(ve.scalar_tensor_tensor(out=y, in0=x_w, scalar=pick(conv_w[w], tile), in1=y,
                                                             op0=ALU.mult, op1=ALU.add))
                each_chunk(dve, self.first, self.count, body, step, 2 * CONV)

        class Sigmoid(Stage):
            def __init__(self, flat, part, silu):
                self.flat, self.part, self.silu = flat, part, silu
                self.n = flat.shape[1] // part
                self.av0, self.vv0 = take("av", self.n), take("vv", self.n)

            def halves(self, i):
                return spare[:, (i % 2) * self.part:(i % 2 + 1) * self.part]

            def scalar(self, act, step):
                for i in range(self.n):
                    if i >= 2:
                        act.wait_ge(vv, self.vv0 + i - 1)
                    se.activation(self.halves(i), self.flat[:, i * self.part:(i + 1) * self.part],
                                  ACT.Exp, scale=-1.0).then_inc(av, 1)

            def vector(self, dve, step):
                for i in range(self.n):
                    dve.wait_ge(av, self.av0 + i + 1)
                    e, a = self.halves(i), self.flat[:, i * self.part:(i + 1) * self.part]
                    step(ve.tensor_scalar(e, e, 1.0, None, ALU.add))
                    if self.silu:
                        step(ve.reciprocal(e, e))
                        ve.tensor_tensor(a, a, e, ALU.mult).then_inc(vv, 1)
                    else:
                        ve.reciprocal(a, e).then_inc(vv, 1)

        class Turn(Stage):
            def __init__(self, tiles, evac, each=4):
                self.tiles, self.evac, self.each = tiles, evac, each
                self.banks = -(-len(tiles) // each)
                self.mm0 = take("mm", self.banks)

            def tensor(self, pe):
                for n, tile in enumerate(self.tiles):
                    k = tile.shape[1]
                    last = te.transpose(psum[0:k, n // self.each, (n % self.each) * P:(n % self.each + 1) * P],
                                        tile, ident)
                    if n % self.each == self.each - 1 or n == len(self.tiles) - 1:
                        last.then_inc(mm, 1)

            def scalar(self, act, step):
                for b in range(self.banks):
                    act.wait_ge(mm, self.mm0 + b + 1)
                    self.evac(b)

        def dt_projection():
            for t in range(NT):
                for k in range(KD):
                    te.matmul(psum[:, 0, t * SH:(t + 1) * SH], normed[:, k, t * P:(t + 1) * P], w_dt[:, k, :],
                              start=(k == 0), stop=(k == KD - 1))

        def dt_bias(step):
            for t in range(NT):
                a = slice(t * SH, (t + 1) * SH)
                step(ve.tensor_tensor(dt[:, a], psum[:, 0, a], row("dt_bias"), ALU.add))
            step(ve.scalar_tensor_tensor(out=dt_tmp, in0=dt, scalar=-1.0, in1=dt, op0=ALU.mult, op1=ALU.min))
            step(ve.tensor_scalar(dt, dt, 0.0, None, ALU.max))

        def dt_softplus(step):
            se.activation(a_exp, row("a_log"), ACT.Exp)
            step(se.activation(dt_tmp, dt_tmp, ACT.Exp))
            se.activation(dt_tmp, dt_tmp, ACT.Ln, bias=1.0)

        def dt_decay(step):
            step(ve.tensor_tensor(dt, dt, dt_tmp, ALU.add))
            for t in range(NT):
                a = slice(t * SH, (t + 1) * SH)
                ve.scalar_tensor_tensor(out=dta[:, a], in0=dt[:, a], scalar=-1.0, in1=a_exp,
                                        op0=ALU.mult, op1=ALU.mult)

        def sum_decay():
            upper = C("upper")[:, 0:P]
            te.matmul(psum[:, 0, 0:SH], upper, dta[:, 0:SH], start=True, stop=True)
            te.matmul(psum[:, 0, SH:2 * SH], ones, dta[:, 0:SH], start=True, stop=False)
            te.matmul(psum[:, 0, SH:2 * SH], upper, dta[:, SH:2 * SH], start=False, stop=True)

        def negate_sums(step):
            ve.tensor_scalar(neg_la, psum[:, 0, 0:2 * SH], -1.0, None, ALU.mult)

        def heads_of(ap):
            return ap.rearrange("p (h d) -> p h d", d=64)

        def per_head(v):
            return v.rearrange("p (h o) -> p h o", o=1).to_broadcast([P, SH, 64])

        def scale_x(step):
            for t in range(NT):
                ve.tensor_tensor(heads_of(xdt[:, t, :]), heads_of(x_tok[:, t, :]),
                                 per_head(dt[:, t * SH:(t + 1) * SH]), ALU.mult)
            for t in range(NT):
                a = heads_of(x_tok[:, t, :])
                ve.tensor_tensor(a, a, per_head(row("d_skip")), ALU.mult)

        def cb_products():
            for g in range(SG):
                for t in range(NT):
                    te.matmul(psum[:, g, t * S:t * S + S - t * P], conv[:, KI + g, t * P:(t + 1) * P],
                              conv[:, KI + SG + g, t * P:S], start=True, stop=True)

        def copy_cb(step):
            for g in range(SG):
                se.copy(cb[:, g, :], psum[:, g, 0:384])

        class Scan(Stage):
            def tensor(self, pe):
                upper = C("upper")
                for h in range(SH + 1):
                    if h < SH:
                        if h >= 2:
                            pe.wait_ge(scan_read, h - 1)
                        te.matmul(psum[:, h % 2, 0:S], dta[:, h:h + 1].to_broadcast([P, P]), upper,
                                  start=True, stop=False)
                        te.matmul(psum[:, h % 2, P:S], dta[:, SH + h:SH + h + 1].to_broadcast([P, P]), upper[:, 0:P],
                                  start=False, stop=True).then_inc(scan_sums, 1)
                    if h >= 1:
                        i = h - 1
                        g = i // SHG
                        pe.wait_ge(scan_masked, i + 1)
                        if i % SHG == 0 and g >= 2:
                            pe.wait_ge(scan_gated, g - 1)
                        m, bank, a = decay[:, i % 2, :], 4 + 2 * (g % 2), slice((i % SHG) * 64, (i % SHG + 1) * 64)
                        xa = slice(i * 64, (i + 1) * 64)
                        te.matmul(psum[:, bank, a], m[:, 0:P], xdt[:, 0, xa], start=True, stop=True)
                        te.matmul(psum[:, bank + 1, a], m[:, P:S], xdt[:, 0, xa], start=True, stop=False)
                        te.matmul(psum[:, bank + 1, a], m[:, S:384], xdt[:, 1, xa], start=False, stop=True
                                  ).then_inc(scan_y, 1)

            def scalar(self, act, step):
                for h in range(SH):
                    act.wait_ge(scan_read, h + 1)
                    se.activation(decay[:, h % 2, :], decay[:, h % 2, :], ACT.Exp).then_inc(scan_exp, 1)

            def vector(self, dve, step):
                causal = C("causal")
                for h in range(SH + 1):
                    if h < SH:
                        dve.wait_ge(scan_sums, h + 1)
                        if h >= 2:
                            dve.wait_ge(scan_y, h - 1)
                        d = decay[:, h % 2, :]
                        ve.scalar_tensor_tensor(out=d[:, 0:S], in0=psum[:, h % 2, 0:S], scalar=neg_la[:, h:h + 1],
                                                in1=causal, op0=ALU.add, op1=ALU.add)
                        ve.scalar_tensor_tensor(out=d[:, S:384], in0=psum[:, h % 2, P:S],
                                                scalar=neg_la[:, SH + h:SH + h + 1], in1=causal[:, 0:P],
                                                op0=ALU.add, op1=ALU.add).then_inc(scan_read, 1)
                    if h >= 1:
                        i = h - 1
                        dve.wait_ge(scan_exp, i + 1)
                        d = decay[:, i % 2, :]
                        ve.tensor_tensor(d, d, cb[:, i // SHG, :], ALU.mult).then_inc(scan_masked, 1)
                        if i % SHG == SHG - 1:
                            g = i // SHG
                            dve.wait_ge(scan_y, i + 1)
                            for t in range(NT):
                                a = slice(g * GW, (g + 1) * GW)
                                y = y_tok[:, t, a]
                                ins = ve.tensor_tensor(y, psum[:, 4 + 2 * (g % 2) + t, :], x_tok[:, t, a], ALU.add)
                                if t == NT - 1:
                                    ins.then_inc(scan_gated, 1)
                                    dve.wait_ge(scan_gated, g + 1)
                                else:
                                    step(ins)
                                step(ve.tensor_tensor(y, y, z1[:, t, a], ALU.mult))
                                n = t * SG + g
                                ve.scalar_tensor_tensor(out=spare[:, 2048:2048 + GW], in0=y, scalar=1.0, in1=y,
                                                        op0=ALU.mult, op1=ALU.mult, accum_out=ssq[:, n:n + 1])

        def mean_square(step):
            ve.tensor_scalar(ssq, ssq, 1.0 / GW, EPS, ALU.mult, ALU.add)

        def inverse_root(step):
            step(se.activation(ssq, ssq, ACT.Ln))
            se.activation(ssq, ssq, ACT.Exp, scale=-0.5)

        def normalise_groups(step):
            for t in range(NT):
                for g in range(SG):
                    y = y_tok[:, t, g * GW:(g + 1) * GW]
                    ve.tensor_scalar(y, y, ssq[:, t * SG + g:t * SG + g + 1], None, ALU.mult)

        def ssm_turned(b):
            for m in range(2):
                se.activation(ssm_t[:, 2 * b + m, :], psum[:, b, m * S:(m + 1) * S], ACT.Copy,
                              scale=col("ssm_norm", 2 * b + m))

        class Branches(Stream):
            def __init__(self):
                self.stream(W["w_branch"], 10, 2 * D // CW)
                self.tmp = spare[:, KD * 2 * S - 512:].rearrange("p (m t) -> p m t", m=2)

            def tensor(self, pe):
                def body(ch):
                    self.begin(pe, ch)
                    half = ch.j % 2
                    attn_bank, ssm_bank = 2 * ((ch.slot - half) % RING), 2 * ((ch.slot + 1 - half) % RING)
                    if half == 0:
                        pe.wait_ge(chunk_free, ch.number + 2)
                    for m in range(2):
                        for k in range(10):
                            row_tile = half * 10 + k
                            x = attn1[:, row_tile, :] if row_tile < 4 else ssm_t[:, row_tile - 4, :]
                            last = te.matmul(psum[:, (attn_bank if row_tile < 4 else ssm_bank) + m, 0:S],
                                             ring[:, ch.slot, k * CW + m * P:k * CW + (m + 1) * P], x,
                                             start=row_tile in (0, 4), stop=row_tile in (3, 19))
                    last.then_inc(chunk_done, 1)
                each_chunk(pe, self.first, self.count, body)

            def vector(self, dve, step):
                def body(ch):
                    if ch.j % 2 == 0:
                        return
                    attn_bank, ssm_bank = 2 * ((ch.slot - 1) % RING), 2 * ch.slot
                    dve.wait_ge(chunk_done, CRED + ch.number + 1)
                    out = merged2[:, bass.ds(ch.index - 1, 2), :]
                    step(ve.tensor_tensor(out, psum[:, attn_bank:attn_bank + 2, 0:S],
                                          gates1[:, bass.ds(ch.index - 1, 2), :], ALU.mult))
                    step(ve.tensor_tensor(self.tmp, psum[:, ssm_bank:ssm_bank + 2, 0:S],
                                          gates1[:, bass.ds(ch.index - 1 + KD, 2), :], ALU.mult))
                    ve.tensor_tensor(out, out, self.tmp, ALU.add).then_inc(chunk_free, 2)
                each_chunk(dve, self.first, self.count, body, step, 1)


        TT = 2 * NT

        class HeadNorm(Stage):
            def __init__(self, items, space):
                self.items = items
                self.av0, self.vv0 = take("av", len(items) + 1), take("vv", 1)
                self.squares, self.stats, at, st = [], [], 0, 576
                for _, tiles, heads, width, *_ in items:
                    self.squares.append(space[:, at:at + tiles * heads * width])
                    self.stats.append(small[:, st:st + tiles * heads])
                    at, st = at + tiles * heads * width, st + tiles * heads
                assert st <= 760 and at <= space.shape[1]
                self.all_stats = small[:, 576:st]

            def scalar(self, act, step):
                for (view, tiles, heads, width, *_), sq in zip(self.items, self.squares):
                    for t in range(tiles):
                        last = se.activation(sq[:, t * heads * width:(t + 1) * heads * width].rearrange(
                            "p (h d) -> p h d", h=heads), view(t), ACT.Square)
                    last.then_inc(av, 1)
                act.wait_ge(vv, self.vv0 + 1)
                step(se.activation(self.all_stats, self.all_stats, ACT.Ln))
                se.activation(self.all_stats, self.all_stats, ACT.Exp, scale=-0.5).then_inc(av, 1)

            def vector(self, dve, step):
                for n, ((_, tiles, heads, width, *_), sq, st) in enumerate(zip(self.items, self.squares, self.stats)):
                    dve.wait_ge(av, self.av0 + n + 1)
                    step(ve.tensor_reduce(st, sq.rearrange("p (h d) -> p h d", d=width), AX.X, ALU.add))
                    ins = ve.tensor_scalar(st, st, 1.0 / width, EPS, ALU.mult, ALU.add)
                    step(ins)
                ve.tensor_copy(self.all_stats, self.all_stats).then_inc(vv, 1)
                dve.wait_ge(av, self.av0 + len(self.items) + 1)
                for n, ((view, tiles, heads, width, gain, rope, out), sq, st) in enumerate(
                        zip(self.items, self.squares, self.stats)):
                    for t in range(tiles):
                        shape = [P, heads, width]
                        r = st[:, t * heads:(t + 1) * heads].rearrange("p (h o) -> p h o", o=1).to_broadcast(shape)
                        if gain is None:
                            ve.tensor_tensor(out(t), view(t), r, ALU.mult)
                            continue
                        g = gain.rearrange("p (o d) -> p o d", o=1).to_broadcast(shape)
                        if rope is None or t >= NT:
                            step(ve.tensor_tensor(view(t), view(t), r, ALU.mult))
                            ve.tensor_tensor(out(t), view(t), g, ALU.mult)
                            continue
                        step(ve.tensor_tensor(view(t), view(t), r, ALU.mult))
                        step(ve.tensor_tensor(view(t), view(t), g, ALU.mult))
                        cos, sin = (C(name)[:, t * width:(t + 1) * width] for name in rope)
                        q = width // 4
                        rot = sq[:, t * heads * width:(t + 1) * heads * width].rearrange("p (h d) -> p h d", h=heads)
                        for axis in range(2):
                            for half in range(2):
                                a, b = (2 * axis + half) * q, (2 * axis + 1 - half) * q
                                s = sin[:, a:a + q].rearrange("p (o d) -> p o d", o=1).to_broadcast([P, heads, q])
                                ins = ve.tensor_tensor(rot[:, :, a:a + q], view(t)[:, :, b:b + q], s, ALU.mult)
                        step(ins)
                        c = cos.rearrange("p (o d) -> p o d", o=1).to_broadcast(shape)
                        step(ve.tensor_tensor(view(t), view(t), c, ALU.mult))
                        ve.tensor_tensor(out(t), view(t), rot, ALU.add)

        def heads_view(a, start, heads, width, pitch=None, off=0):
            pitch = pitch or width
            return lambda t: a[:, t, start:start + heads * pitch].rearrange(
                "p (h d) -> p h d", d=pitch)[:, :, off:off + width]

        AQ, BQ, AK, AV, BK, BV = 0, 512, 1024, 1152, 1280, 1792
        ab = arena[:, 0:TT * 2304].rearrange("p (t n) -> p t n", t=TT)
        q2 = arena[:, 9216:9216 + 8 * 512].rearrange("p (m t) -> p m t", t=512)
        k2 = arena[:, 13312:13312 + 5 * 512].rearrange("p (m t) -> p m t", t=512)
        lam = small[:, 104:105]
        lam_tmp = small[:, 106:108]
        lam_prod = work[:, 10240:10240 + HD]
        rope64, rope32 = ("cos64", "sin64"), ("cos32", "sin32")

        def lambda_dots(step):
            for n, (a, b) in enumerate((("lq1", "lk1"), ("lq2", "lk2"))):
                step(ve.tensor_tensor(lam_prod, row(a), row(b), ALU.mult))
                step(ve.tensor_reduce(lam_tmp[:, n:n + 1], lam_prod, AX.X, ALU.add))

        def lambda_exp(step):
            se.activation(lam_tmp, lam_tmp, ACT.Exp)

        def lambda_sum(step):
            step(ve.tensor_tensor(lam, lam_tmp[:, 0:1], lam_tmp[:, 1:2], ALU.subtract))
            step(ve.tensor_scalar(lam, lam, 0.8 - 0.6, None, ALU.add))

        def ab_units():
            units = []
            for t in range(TT):
                ctx_only = t >= NT
                keys = slice(S, 2 * S) if ctx_only else slice(0, 2 * S)
                key_tiles = range(NT, TT) if ctx_only else range(TT)
                for h in range(8):
                    side, pair = h // 4, h % 4
                    a = slice(side * HD, (side + 1) * HD)
                    biases = [(S, None)] if ctx_only else [(S, C("window")[:, t * S:(t + 1) * S]), (S, None)]
                    m = Map([(q2[a, pair, t * P:(t + 1) * P], k2[a, 0, keys])], biases, row("sink")[:, h:h + 1])
                    units.append(Unit([m], [ab[:, kt, AV + side * HD:AV + (side + 1) * HD] for kt in key_tiles],
                                      normed[(h % 2) * HD:(h % 2 + 1) * HD, h // 2, t * P:(t + 1) * P], HD ** -0.5))
                for h in range(4):
                    maps = []
                    for m in range(2):
                        a = slice(m * HD, (m + 1) * HD)
                        maps.append(Map([(q2[a, 4 + h, t * P:(t + 1) * P], k2[a, 1 + h, keys])],
                                        [(len(key_tiles) * P, None)]))
                    units.append(Unit(maps, [ab[:, kt, BV + h * P:BV + (h + 1) * P] for kt in key_tiles],
                                      normed[:, 4 + h, t * P:(t + 1) * P], HD ** -0.5, lam))
            return units

        class SubNorm(Stage):
            def __init__(self):
                self.av0, self.vv0, self.mm0 = take("av", 2), take("vv", 1), take("mm", 1)
                self.y = normed[:, 4:8, :].rearrange("p k t -> p (k t)")
                self.sq, self.r, self.fits = work[:, 0:2048], work[:, 2048:4096], work[:, 4096:6144]

            def tensor(self, pe):
                pe.wait_ge(av, self.av0 + 1)
                for h in range(4):
                    last = te.matmul(psum[:, h, :], ones, self.sq[:, h * 512:(h + 1) * 512], start=True, stop=True)
                last.then_inc(mm, 1)

            def scalar(self, act, step):
                se.activation(self.sq, self.y, ACT.Square, scale=2.0 ** -20).then_inc(av, 1)
                act.wait_ge(vv, self.vv0 + 1)
                se.activation(self.r, self.r, ACT.Sqrt).then_inc(av, 1)

            def vector(self, dve, step):
                total = psum[:, 0:4, :].rearrange("p b n -> p (b n)")
                largest = float(np.finfo(np.float32).max) * 2.0 ** -40
                dve.wait_ge(mm, self.mm0 + 1)
                step(ve.tensor_scalar(self.r, total, 1.0 / P, EPS * 2.0 ** -40, ALU.mult, ALU.add))
                step(ve.tensor_scalar(self.fits, total, largest, None, ALU.is_le))
                ve.tensor_scalar(self.r, self.r, 2.0 ** 100, None, ALU.min).then_inc(vv, 1)
                dve.wait_ge(av, self.av0 + 2)
                step(ve.reciprocal(self.r, self.r))
                step(ve.scalar_tensor_tensor(out=self.r, in0=self.r, scalar=(1.0 - (0.8 - 0.6)) * 2.0 ** -20,
                                             in1=self.fits, op0=ALU.mult, op1=ALU.mult))
                ve.scalar_tensor_tensor(out=self.y, in0=self.y, scalar=col("b_sub"), in1=self.r,
                                        op0=ALU.mult, op1=ALU.mult)

        cdq = arena[:, 0:NT * 1280].rearrange("p (t n) -> p t n", t=NT)
        cdk = arena[:, 2560:2560 + TT * 1280].rearrange("p (t n) -> p t n", t=TT)
        kr = arena[:, 7680:7680 + TT * ROPE].rearrange("p (t n) -> p t n", t=TT)
        dq_t = arena[:, 7808:7808 + 4 * S].rearrange("p (m t) -> p m t", t=S)
        dk_t = arena[:, 8832:8832 + 4 * 512].rearrange("p (m t) -> p m t", t=512)
        cq_t = arena[:, 10880:10880 + 6 * S].rearrange("p (m t) -> p m t", t=S)
        ckv_t = arena[:, 12416:12416 + 2 * 512].rearrange("p (m t) -> p m t", t=512)
        mq = arena[:, 13440:13440 + NT * 8 * MQ].rearrange("p (t n) -> p t n", t=NT)
        mq_t = arena[:, 0:8 * S].rearrange("p (m t) -> p m t", t=S)
        mk_t = arena[:, 2560:2560 + 8 * 512].rearrange("p (m t) -> p m t", t=512)
        kv = work[:, 2048:2048 + TT * 1024].rearrange("p (t n) -> p t n", t=TT)
        mk = work[:, 6144:6144 + TT * 8 * MQ].rearrange("p (t n) -> p t n", t=TT)
        grid_bias = work[:, 2048:2048 + 8 * NT * S].rearrange("p (h t n) -> p h t n", h=8, t=NT)

        def kr_projection():
            for t in range(TT):
                for k in range(KD):
                    te.matmul(psum[:, 0, t * ROPE:(t + 1) * ROPE], normed[:, k, t * P:(t + 1) * P], w_kr[:, k, :],
                              start=(k == 0), stop=(k == KD - 1))

        def copy_kr(step):
            se.copy(arena[:, 7680:7680 + TT * ROPE], psum[:, 0, 0:TT * ROPE])

        def spread_kr(step):
            for t in range(TT):
                ve.tensor_copy(heads_view(mk, 0, 8, ROPE, MQ, HD)(t), heads_view(kr, 0, 1, ROPE)(t).to_broadcast(
                    [P, 8, ROPE]))

        def grid_bias_stage():
            loads = []
            for t in range(NT):
                for rl in range(2):
                    for h in range(8):
                        dst = grid_bias[rl * GRID_W:(rl + 1) * GRID_W, h, t, :].rearrange("p (j k) -> p j k", j=ROWS)
                        start = (h * RPB_R + WIN_ROWS - 1 - 2 * t - rl) * RPB_PAD
                        loads.append((dst, bass.AP(scratch_rpb.tensor, start,
                                                   [[1, GRID_W], [RPB_PAD, ROWS], [1, GRID_W]])))
            return Mirror(grid_bias.rearrange("p h t n -> p (h t n)"), C("mirror64"), loads, C("colmask"))

        def grid_units():
            units = []
            for t in range(NT):
                for h in range(8):
                    a = slice((h % 2) * HD, (h % 2 + 1) * HD)
                    m = Map([(dq_t[a, h // 2, t * P:(t + 1) * P], dk_t[a, h // 2, :])],
                            [(S, grid_bias[:, h, t, :]), (S, None)])
                    units.append(Unit([m], [cdk[:, kt, 768 + h * HD:768 + (h + 1) * HD] for kt in range(TT)],
                                      normed[a, 4 + h // 2, t * P:(t + 1) * P], HD ** -0.5))
            return units

        def cq_turned(b):
            for m in range(2):
                se.activation(cq_t[:, 2 * b + m, :], psum[:, b, m * S:(m + 1) * S], ACT.Copy,
                              scale=col("cq_norm", 2 * b + m))

        def mla_units():
            units = []
            for t in range(NT):
                for h in range(8):
                    m = Map([(mq_t[0:MQ, h, t * P:(t + 1) * P], mk_t[0:MQ, h, :])], [(2 * S, None)])
                    units.append(Unit([m], [kv[:, kt, h * P + HD:(h + 1) * P] for kt in range(TT)],
                                      normed[(h % 2) * HD:(h % 2 + 1) * HD, h // 2, t * P:(t + 1) * P], MQ ** -0.5))
            return units

        result = work[:, 0:NT * D].rearrange("p (t n) -> p t n", t=NT)

        class Store(Stage):
            def sync(self, sp):
                sp.wait_ge(stage_end, 3 * stages.index(self))
                sp.dma_start(out[0].rearrange("(t p) n -> p t n", p=P), result).then_inc(out_done, 16)
                sp.wait_ge(out_done, 16)

        stages = [Setup(), Modulation(0), Modulation(1)]
        stages += [
            Norm(S, lambda k, s: col("norm1", k), None, normed),
            LinearF(W["w_qk"], KD, 12, normed, S, qk1),
            LinearT(W["w_v"], KD, AW // CW, normed, NT, v1),
            relative_bias(),
            Attention(attention1_units(), work),
            ConvX(),
            LinearT(W["w_z"], KD, DI // CW, normed, NT, z1),
            LinearF(W["w_g"], KD, 2 * D // CW, normed, S, gates1),
            Only("tensor", dt_projection),
            Only("vector", dt_bias),
            Only("scalar", dt_softplus),
            Only("vector", dt_decay),
            Only("tensor", sum_decay),
            Only("vector", negate_sums),
            Sigmoid(conv[:].rearrange("p m t -> p (m t)"), 1536, True),
            Sigmoid(z1[:].rearrange("p t n -> p (t n)"), 1024, True),
            Sigmoid(gates1[:].rearrange("p m t -> p (m t)"), 1024, False),
            Turn([conv[:, 4 * (n // 4 % 4) + n % 4, (n // 16) * P:(n // 16 + 1) * P] for n in range(2 * KI)],
                 lambda b: se.copy(x_tok[:, b // 4, (b % 4) * 512:(b % 4 + 1) * 512], psum[:, b, :])),
            Only("tensor", cb_products),
            Only("scalar", copy_cb),
            Only("vector", scale_x),
            Scan(),
            Only("vector", mean_square),
            Only("scalar", inverse_root),
            Only("vector", normalise_groups),
            Turn([y_tok[:, t, k * P:(k + 1) * P] for k in range(KI) for t in range(NT)], ssm_turned),
            Branches(),
            LinearF(W["w_out"], KD, D // CW, merged2, S, None, into_resid=True),
            Norm(S, lambda k, s: col("norm2", k), None, normed),
            FfnUp(W["w_gu"], S), FfnDown(W["w_down"], S, None),
            Norm(S, lambda k, s: col("final", k), None, resid),
        ]
        every = 2 * S
        stages += [
            modulated(0, 0, 1, every), FfnUp(W["w_gu10"], every), FfnDown(W["w_down10"], every, (0, 2)),
            modulated(0, 3, 4, every),
            LinearT(W["w_ab"], KD, 2304 // CW, normed, TT, ab),
            HeadNorm([(heads_view(ab, start, heads, HD), TT, heads, HD, row(gain), rope64,
                       heads_view(ab, start, heads, HD))
                      for start, heads, gain in ((AQ, 8, "aq"), (BQ, 8, "bq"), (AK, 2, "ak"), (BK, 8, "bk"))], work),
            Turn([ab[:, t, m * P:(m + 1) * P] for m in range(8) for t in range(TT)],
                 lambda b: se.copy(q2[:, b, :], psum[:, b, :])),
            Turn([ab[:, t, c:c + P] for c in (AK, *range(BK, BV, P)) for t in range(TT)],
                 lambda b: se.copy(k2[:, b, :], psum[:, b, :])),
            Only("vector", lambda_dots), Only("scalar", lambda_exp), Only("vector", lambda_sum),
            Attention(ab_units(), work),
            SubNorm(),
            LinearF(W["w_ab_out"], KD, D // CW, normed, every, None, into_resid=True, gate=(0, 5)),
            modulated(0, 6, 7, every), FfnUp(W["w_gu20"], every), FfnDown(W["w_down20"], every, (0, 8)),
            modulated(1, 0, 1, every), FfnUp(W["w_gu11"], every), FfnDown(W["w_down11"], every, (1, 2)),
            modulated(1, 3, 4, every),
            LinearT(W["w_cdq"], KD, 1280 // CW, normed, NT, cdq),
            LinearT(W["w_cdk"], KD, 1280 // CW, normed, TT, cdk),
            Only("tensor", kr_projection), Only("scalar", copy_kr),
            HeadNorm([(heads_view(cdq, QR, 8, HD), NT, 8, HD, row("dq"), None, heads_view(cdq, QR, 8, HD)),
                      (heads_view(cdk, KVR, 8, HD), TT, 8, HD, row("dk"), None, heads_view(cdk, KVR, 8, HD)),
                      (heads_view(cdq, 0, 1, QR), NT, 1, QR, None, None, heads_view(cdq, 0, 1, QR)),
                      (heads_view(cdk, 0, 1, KVR), TT, 1, KVR, None, None, heads_view(cdk, 0, 1, KVR))], work),
            Turn([cdq[:, t, QR + m * P:QR + (m + 1) * P] for m in range(4) for t in range(NT)],
                 lambda b: se.copy(dq_t[:, 2 * b:2 * b + 2, :].rearrange("p m t -> p (m t)"), psum[:, b, :])),
            Turn([cdk[:, t, KVR + m * P:KVR + (m + 1) * P] for m in range(4) for t in range(TT)],
                 lambda b: se.copy(dk_t[:, b, :], psum[:, b, :])),
            Turn([cdq[:, t, m * P:(m + 1) * P] for m in range(6) for t in range(NT)], cq_turned),
            Turn([cdk[:, t, m * P:(m + 1) * P] for m in range(2) for t in range(TT)],
                 lambda b: se.activation(ckv_t[:, b, :], psum[:, b, :], ACT.Copy, scale=col("ckv_norm", b))),
            grid_bias_stage(),
            Attention(grid_units(), work[:, 0:2048]),
            LinearT(W["w_uq"], QR // P, 3, cq_t, NT, mq),
            LinearT(W["w_ukv"], KVR // P, 4, ckv_t, TT, kv),
            HeadNorm([(heads_view(mq, 0, 8, HD, MQ), NT, 8, HD, row("cqn"), None, heads_view(mq, 0, 8, HD, MQ)),
                      (heads_view(mq, 0, 8, ROPE, MQ, HD), NT, 8, ROPE, row("cqr"), rope32,
                       heads_view(mq, 0, 8, ROPE, MQ, HD))], work[:, 0:2048]),
            HeadNorm([(heads_view(kv, 0, 8, HD, P), TT, 8, HD, row("ckn"), None, heads_view(mk, 0, 8, HD, MQ)),
                      ], work[:, 0:2048]),
            HeadNorm([(heads_view(kr, 0, 1, ROPE), TT, 1, ROPE, row("ckr"), rope32, heads_view(kr, 0, 1, ROPE))],
                     work[:, 0:2048]),
            Only("vector", spread_kr),
            Turn([mq[:, t, h * MQ:(h + 1) * MQ] for h in range(8) for t in range(NT)],
                 lambda b: se.copy(mq_t[0:MQ, 2 * b:2 * b + 2, :].rearrange("p m t -> p (m t)"), psum[0:MQ, b, :])),
            Turn([mk[:, t, h * MQ:(h + 1) * MQ] for h in range(8) for t in range(TT)],
                 lambda b: se.copy(mk_t[0:MQ, b, :], psum[0:MQ, b, :])),
            Attention(mla_units(), work[:, 0:2048]),
            LinearF(W["w_cd_out"], KD, D // CW, normed, S, None, into_resid=True, gate=(1, 5)),
            modulated(1, 6, 7, S), FfnUp(W["w_gu21"], S), FfnDown(W["w_down21"], S, (1, 8)),
            Turn([resid[:, k, t * P:(t + 1) * P] for t in range(NT) for k in range(KD)],
                 lambda b: se.copy(result[:, b // 2, (b % 2) * 512:(b % 2 + 1) * 512], psum[:, b, :])),
            Store(),
        ]

        n_end = [0]

        def run(engine, name, step=None):
            for n, st in enumerate(stages):
                f = {"tensor": st.tensor, "scalar": st.scalar, "vector": st.vector}[name]
                f(engine, step) if step else f(engine)
                engine.drain().then_inc(stage_end, 1)
                engine.wait_ge(stage_end, 3 * (n + 1))

        @block.sync
        def _(sp):
            for st in stages:
                st.sync(sp)
            if taps:
                sp.wait_ge(stage_end, 3 * len(stages))
                named = {"resid": resid, "mod": mod, "arena": arena, "hidden": hidden, "small": small, "normed": normed}
                for n, _ in taps:
                    t = named[n][:]
                    o = nc.dram_tensor("tap_" + n, t.shape, F32, kind="ExternalOutput").ap()
                    sp.dma_start(o, t).then_inc(out_done, 16)
                sp.wait_ge(out_done, 16 * len(taps))

        @block.tensor
        def _(pe):
            run(pe, "tensor")

        @block.scalar
        def _(act):
            run(act, "scalar", Steps(act, act_step))

        @block.vector
        def _(dve):
            run(dve, "vector", Steps(dve, dve_step))



def chunked(w, rows=None):
    k, m = w.shape
    rows = rows or k // P
    a = w.reshape(k // (rows * P), rows, P, m // CW, CW)
    return a.transpose(3, 0, 2, 1, 4).reshape(-1, P, rows * CW)


def feature_major(v):
    return v.reshape(-1, P).T


def lay_out(x):
    w_in = x["w_in"][0]
    cuts = np.cumsum([AW, AW, AW, DI, XBC, SH, 2 * D])
    wq, wk, wv, wz, wx, wdt, wg = (w_in[:, a:b] for a, b in zip([0, *cuts[:-1]], cuts))
    cd = x["cd_w_in_2"][0]
    cc = np.cumsum([QR, 512, KVR, ROPE, 512, 512])
    c_q, c_dq, c_kv, c_kr, c_dk, c_dv = (cd[:, a:b] for a, b in zip([0, *cc[:-1]], cc))
    ab = x["ab_w_in_2"][0]
    aq = ab[:, :512].reshape(D, 2, 4, HD).transpose(0, 2, 1, 3).reshape(D, 512)
    ab = np.concatenate([aq, ab[:, 512:]], 1)
    gate1, up1 = chunked(x["w_ffn_in"][0][:, :FF]), chunked(x["w_ffn_in"][0][:, FF:])

    def alternate(a, b):
        return np.stack([a, b], 1).reshape(2 * a.shape[0], *a.shape[1:])

    a, s = x["w_attn_branch"][0], x["w_ssm_branch"][0]
    a, s = (w.reshape(w.shape[0] // P, P, D // CW, CW) for w in (a, s))
    branch = np.concatenate([a, s], 0)
    branch = branch.reshape(2, 10, P, D // CW, CW).transpose(3, 0, 2, 1, 4).reshape(-1, P, 10 * CW)
    out = {
        "x": x["x"][0].T.reshape(KD, P, S).transpose(1, 0, 2),
        "ctx": x["ctx_2"][0].T.reshape(KD, P, S).transpose(1, 0, 2),
        "w_qk": np.concatenate([chunked(wq), chunked(wk)]), "w_v": chunked(wv), "w_z": chunked(wz),
        "w_x": chunked(wx), "w_g": chunked(wg),
        "w_dt": wdt.reshape(KD, P, SH).transpose(1, 0, 2),
        "w_kr": c_kr.reshape(KD, P, ROPE).transpose(1, 0, 2),
        "w_branch": branch, "w_out": chunked(x["w_out"][0]),
        "w_gu": alternate(gate1, up1), "w_down": chunked(x["w_ffn_out"][0], KF // 2),
        "w_mod": np.concatenate([chunked(w) for w in x["w_mod_2"]]),
        "w_ab": chunked(ab), "w_ab_out": chunked(x["ab_w_out_2"][0]),
        "w_cdq": np.concatenate([chunked(c_q), chunked(c_dq)]),
        "w_cdk": np.concatenate([chunked(c_kv), chunked(c_dk), chunked(c_dv)]),
        "w_uq": chunked(x["c_w_uq_2"][0]), "w_ukv": chunked(x["c_w_ukv_2"][0]),
        "w_cd_out": chunked(x["cd_w_out_2"][0]),
        "rel_bias": x["rel_bias"], "rpb": x["d_rpb_2"][0].reshape(8 * RPB_R, RPB_C),
    }
    for n in (1, 2):
        for layer in range(LAYERS):
            out[f"w_gu{n}{layer}"] = alternate(chunked(x[f"ffn{n}_w_gate_2"][layer]), chunked(x[f"ffn{n}_w_up_2"][layer]))
            out[f"w_down{n}{layer}"] = chunked(x[f"ffn{n}_w_down_2"][layer], KF // 2)
    cond = np.stack([feature_major(x["c_2"][0]), feature_major(x["c_ctx_2"])], 2).reshape(P, 2 * KD)
    vectors = {
        "norm1": feature_major(x["norm1_w"][0]), "norm2": feature_major(x["norm2_w"][0]),
        "final": feature_major(x["final_norm_w"]),
        "conv_w": np.concatenate([feature_major(r) for r in x["conv_w"][0]], 1),
        "conv_b": feature_major(x["conv_b"][0]), "ssm_norm": feature_major(x["ssm_norm_w"][0]),
        "b_mod": feature_major(x["b_mod_2"].reshape(-1)), "cond": cond, "b_sub": feature_major(x["b_sub_norm_2"][0]),
        "cq_norm": feature_major(x["c_q_a_norm_2"][0]), "ckv_norm": feature_major(x["c_kv_a_norm_2"][0]),
    }
    out["cols"] = np.concatenate([vectors[n] for n in COLS], 1)
    names = ("dt_bias", "a_log", "d_skip", "a_q_norm_2", "a_k_norm_2", "b_q_norm_2", "b_k_norm_2", "d_q_norm_2",
             "d_k_norm_2", "c_q_nope_norm_2", "c_q_rope_norm_2", "c_k_nope_norm_2", "c_k_rope_norm_2", "a_sink_2",
             "b_lambda_q1_2", "b_lambda_k1_2", "b_lambda_q2_2", "b_lambda_k2_2")
    out["rowv"] = np.concatenate([x[n][0] for n in names])[None]
    return out


def kernel(**inputs):
    import concourse.bacc as bacc
    from concourse.bass_utils import run_bass_kernel_spmd

    nc = bacc.Bacc("TRN2", target_bir_lowering=False, num_devices=1)
    laid = lay_out({name: np.asarray(a) for name, a in inputs.items()})
    consts, where = shape_constants()
    laid["consts"] = consts
    arrays = {"in_" + name: np.ascontiguousarray(a) for name, a in laid.items()}
    W = {name: nc.dram_tensor("in_" + name, a.shape, F32, kind="ExternalInput").ap() for name, a in laid.items()}
    out = nc.dram_tensor("out_0", (1, S, D), F32, kind="ExternalOutput").ap()
    build(nc, W, W["consts"], where, out)
    r = run_bass_kernel_spmd(nc, [arrays], core_ids=[0])
    return r.results[0]["out_0"]
```

```python
from contextlib import ExitStack

import numpy as np

import concourse.bass as bass
from concourse import mybir

ALU = mybir.AluOpType
ACT = mybir.ActivationFunctionType
F32 = mybir.dt.float32
F32R = mybir.dt.float32r
AX = mybir.AxisListType

P = 128
S = 256
NT = S // P
D = 1024
KD = D // P
HD = 64
EPS = 1e-6
NEG = -1e30

DILATIONS = (1, 4, 16)
WINDOWS = (128, 512, 2048)
NG = len(DILATIONS)
HG = 8
AW = NG * HG * HD
N_BUCKETS, REL_MAX = 32, 2048

DI = 2 * D
KI = DI // P
SH = DI // 64
SG = 4
SHG = SH // SG
GW = DI // SG
CONV = 4
XBC = DI + 2 * SG * 128
KX = XBC // P

FF = 2816
KF = FF // P
NMOD = 9
LAYERS = 2

FW = P
TW = 256
KH = KF // 2
RING = 4
SLOT = KH * FW
LEAD = 2
CRED = RING
ARENA = 21760

GRID_W, WIN_COLS, WIN_ROWS = 64, 16, 8
ROWS = S // GRID_W
RPB_R, RPB_C = 2 * WIN_ROWS - 1, 2 * WIN_COLS - 1
RPB_PAD = 2 * GRID_W - 1

QR, KVR, ROPE = 768, 256, 32
MQ = HD + ROPE

TOEP = 3 * P - 1



def bucket(dist):
    exact = N_BUCKETS // 2
    d = np.maximum(dist, 1).astype(np.float32)
    large = exact + (np.log(d / np.float32(exact)) / np.float32(np.log(REL_MAX / exact))
                     * np.float32(N_BUCKETS - exact)).astype(np.int32)
    return np.where(dist < exact, dist, np.minimum(large, N_BUCKETS - 1))


def rope_rows(width):
    nf = width // 4
    inv = (np.float32(10000.0) ** (-np.arange(nf, dtype=np.float32) / np.float32(nf))).astype(np.float32)
    t = np.arange(S)
    out_c, out_s = np.zeros((S, 2, 2, nf), np.float32), np.zeros((S, 2, 2, nf), np.float32)
    for axis, pos in enumerate((t // GRID_W, t % GRID_W)):
        ang = (pos.astype(np.float32)[:, None] * inv).astype(np.float32)
        out_c[:, axis] = np.cos(ang)[:, None]
        out_s[:, axis, 0], out_s[:, axis, 1] = -np.sin(ang), np.sin(ang)
    return out_c.reshape(S, width), out_s.reshape(S, width)


def by_tile(a):
    return a.reshape(NT, P, -1).transpose(1, 0, 2).reshape(P, -1)


def shape_constants():
    p = np.arange(P)
    i, j = np.arange(S)[:, None], np.arange(S)[None]
    c64, s64 = rope_rows(HD)
    c32, s32 = rope_rows(ROPE)
    upper = (p[:, None] <= p[None]).astype(np.float32)
    dist = TOEP - 1 - np.arange(TOEP) - (P - 1)
    onehot = np.zeros((P, TOEP), np.float32)
    onehot[bucket(np.maximum(dist, 0)), np.arange(TOEP)] = 1
    relmask = np.zeros((P, TOEP), np.float32)
    for g, (dil, win) in enumerate(zip(DILATIONS, WINDOWS)):
        ok = (dist >= 0) & (dist <= win) & (dist % dil == 0)
        relmask[g * HG:(g + 1) * HG] = np.where(ok, 0, NEG)
    col = np.arange(GRID_W)
    first = np.clip(col - WIN_COLS // 2, 0, GRID_W - WIN_COLS)
    inside = (col[None] >= first[:, None]) & (col[None] < first[:, None] + WIN_COLS)
    parts = {
        "ident": np.eye(P, dtype=np.float32),
        "mirror": np.eye(P, dtype=np.float32)[::-1],
        "mirror64": np.kron(np.eye(2, dtype=np.float32), np.eye(GRID_W, dtype=np.float32)[::-1]),
        "ones": np.ones((P, P), np.float32),
        "upper": np.concatenate([upper, np.ones((P, P), np.float32)], 1),
        "causal": np.concatenate([np.where(upper > 0, 0, NEG).astype(np.float32), np.zeros((P, P), np.float32)], 1),
        "window": by_tile(np.where(abs(i - j) <= 128, 0, NEG).astype(np.float32)),
        "colmask": np.tile(np.where(inside, 0, NEG).astype(np.float32), (2, ROWS)),
        "cos64": by_tile(c64), "sin64": by_tile(s64), "cos32": by_tile(c32), "sin32": by_tile(s32),
        "onehot": onehot, "relmask": relmask,
    }
    where, at = {}, 0
    for name, a in parts.items():
        where[name] = (at, a.shape[1])
        at += a.shape[1]
    return np.concatenate(list(parts.values()), 1).astype(np.float32), where


COLS = {}
for _name, _n in (("norm1", KD), ("norm2", KD), ("final", KD), ("conv_w", CONV * KX), ("conv_b", KX),
                  ("ssm_norm", KI), ("b_mod", LAYERS * NMOD * KD), ("cond", 2 * KD), ("b_sub", 1),
                  ("cq_norm", QR // P), ("ckv_norm", KVR // P)):
    COLS[_name] = (sum(n for _, n in COLS.values()), _n)
ROWV = {}
for _name, _n in (("dt_bias", SH), ("a_log", SH), ("d_skip", SH), ("aq", HD), ("ak", HD), ("bq", HD), ("bk", HD),
                  ("dq", HD), ("dk", HD), ("cqn", HD), ("cqr", ROPE), ("ckn", HD), ("ckr", ROPE), ("sink", 8),
                  ("lq1", HD), ("lk1", HD), ("lq2", HD), ("lk2", HD)):
    ROWV[_name] = (sum(n for _, n in ROWV.values()), _n)
N_COLS, N_ROWV = sum(n for _, n in COLS.values()), sum(n for _, n in ROWV.values())



class Steps:

    def __init__(self, engine, sem):
        self.engine, self.sem, self.done, self.loop = engine, sem, 0, 0

    def __call__(self, instruction):
        instruction.then_inc(self.sem, 1)
        self.done += 1
        self.engine.wait_ge(self.sem, self.loop + self.done)


class Chunk:

    def __init__(self, first, i, j):
        at = first + j
        self.args = first, i, j
        self.index = RING * i + j
        self.half_index = 2 * i + j // 2
        self.j = j % RING
        self.slot = at % RING
        self.landed = 16 * i + 16 * (at // RING + 1)
        self.number = RING * i + at
        self.bank = 2 * self.slot

    def ahead(self, n):
        first, i, j = self.args
        return Chunk(first, i, j + n)


def each_chunk(engine, first, count, body, steps=None, per_chunk=0, keep=0):
    loops = (count - keep) // RING
    if loops < 2:
        loops = 0
    if loops:
        start = steps.done if steps else 0
        with engine.Fori(0, loops) as i:
            if steps:
                steps.loop = i * int(RING * per_chunk)
            for j in range(RING):
                body(Chunk(first, i, j))
        if steps:
            assert steps.done == start + int(RING * per_chunk)
            steps.loop, steps.done = 0, start + loops * int(RING * per_chunk)
    for j in range(loops * RING, count):
        body(Chunk(first, 0, j))


def pick(ap3, index):
    return ap3[:, bass.ds(index, 1), :].rearrange("p a n -> p (a n)")


def build(nc, W, consts, where, out):
    with ExitStack() as ctx:
        def sb(name, *free):
            return ctx.enter_context(nc.sbuf_tensor(name, [P, *free], F32))

        def sem(name):
            return ctx.enter_context(nc.semaphore(name))

        arena_at = -(-nc.sbuf_base // 32) * 32
        arena = ctx.enter_context(nc.sbuf_tensor("arena", [P, ARENA], F32))

        def at(start, *free):
            n = int(np.prod(free))
            assert start + n <= ARENA
            names = " ".join("abc"[:len(free)])
            return arena[:, start:start + n] if len(free) == 1 else arena[:, start:start + n].rearrange(
                f"p ({names}) -> p {names}", **dict(zip("abc", free)))

        def split_at(name, starts, *free):
            return [nc.alloc_sbuf_tensor_at(name + part, [P, *free], F32R, offset=arena_at + 4 * start)
                    for part, start in zip(("_hi", "_lo"), starts)]

        def split(name, *free):
            return [ctx.enter_context(nc.sbuf_tensor(name + part, [P, *free], F32R)) for part in ("_hi", "_lo")]

        raw = sb("weights_raw", RING, SLOT)
        w_hi, w_lo = split("weights", RING, SLOT)
        normed = split("normed", KD, 2 * S)
        resid = sb("resid", KD, 2 * S)
        const = sb("const", where["onehot"][0])
        cols = sb("cols", N_COLS)
        rowv = sb("rowv", N_ROWV)
        mod = sb("mod", LAYERS * NMOD * KD, 2)
        small = sb("small", 768)
        w_dt = sb("w_dt", KD, SH)
        w_kr = sb("w_kr", KD, ROPE)
        rstd = sb("rstd", 2 * S)
        psum = ctx.enter_context(nc.psum_tensor("psum", [P, 8, 512], F32))
        banks = psum[:].rearrange("p b n -> p (b n)")

        cond = split("cond", 2 * KD)

        hidden = split_at("hidden", (0, KH * 512), KH, 512)
        norm_sq, norm_tmp = at(2 * KH * 512, KD, 512), at(2 * KH * 512 + KD * 512, KD, 512)
        ffn_tmp = at(2 * KH * 512, 2, 2, 512)

        def C(name):
            a, n = where[name]
            return const[:, a:a + n]

        def col(name, k=0, n=1):
            a = COLS[name][0] + k
            return cols[:, a:a + n]

        def row(name):
            a, n = ROWV[name]
            return rowv[:, a:a + n]

        ident = C("ident")
        ones = C("ones")

        landed = [sem(f"weights_landed_{s}") for s in range(RING)]
        chunk_done = sem("chunk_done")
        chunk_free = sem("chunk_free")
        hi_ready = sem("weights_hi_ready")
        lo_ready = sem("weights_lo_ready")
        stage_end = sem("stage_end")
        const_in = sem("constants_landed")
        bias_in = sem("bias_landed")
        bias_rows = sem("bias_rows_ready")
        act_step, dve_step = sem("act_step"), sem("dve_step")
        mm = sem("tensor_ready")
        av = sem("scalar_ready")
        vv = sem("vector_ready")
        out_done = sem("output_written")
        at_scores, at_read, at_max, at_exp, at_probs, at_turned, at_copied, at_pv, at_out = (
            sem("attn_" + n) for n in ("scores_ready", "scores_read", "max_ready", "exp_ready", "probs_ready",
                                       "probs_turned", "turned_copied", "values_ready", "values_read"))

        scan_sums, scan_read, scan_exp, scan_masked, scan_y, scan_gated = (
            sem("scan_" + n) for n in ("sums_ready", "sums_read", "exp_ready", "masked_ready", "y_ready", "y_read"))

        block = ctx.enter_context(nc.Block())
        te, ve, se, ge = nc.tensor, nc.vector, nc.scalar, nc.gpsimd

        counts = {"mm": 0, "av": 0, "vv": 0, "chunks": 0, "units": 0, "bias": 48}

        def take(name, n):
            counts[name] += n
            return counts[name] - n

        scratch_rel = nc.dram_tensor("scratch_rel", (NG * HG, TOEP), F32, kind="Internal").ap()
        scratch_rpb = nc.dram_tensor("scratch_rpb", (8 * RPB_R, RPB_PAD), F32, kind="Internal").ap()


        class Stage:
            def sync(self, sp): pass
            def tensor(self, pe): pass
            def scalar(self, act, step): pass
            def vector(self, dve, step): pass

        class Stream(Stage):
            def stream(self, weights, rows, width, count):
                self.weights, self.size, self.count = weights, rows * width, count
                self.rows, self.width = rows, width
                self.first = take("chunks", count)

            def sync(self, sp):
                def load(ch):
                    sp.wait_ge(lo_ready, ch.number + 1)
                    sp.dma_start(raw[:, ch.slot, 0:self.size],
                                 self.weights[bass.ds(ch.index, 1)].rearrange("a p n -> p (a n)")
                                 ).then_inc(landed[ch.slot], 16)
                each_chunk(sp, self.first, self.count, load)

            def begin(self, pe, ch):
                pe.wait_ge(lo_ready, CRED + ch.number + 1)
                pe.wait_ge(chunk_free, ch.number + 1)

            def product(self, out, ch, weight_cols, weight_is_moving, x_hi, x_lo, start, stop):
                hi, lo = w_hi[:, ch.slot, weight_cols], w_lo[:, ch.slot, weight_cols]
                for n, (w, x) in enumerate(((hi, x_hi), (hi, x_lo), (lo, x_hi))):
                    a, b = (x, w) if weight_is_moving else (w, x)
                    last = te.matmul(out, a, b, start=start and n == 0, stop=stop and n == 2)
                return last

            def split_hi(self, act, ch):
                act.wait_ge(landed[ch.slot], ch.landed)
                act.wait_ge(chunk_done, ch.number + 1)
                se.copy(w_hi[:, ch.slot, 0:self.size], raw[:, ch.slot, 0:self.size]).then_inc(hi_ready, 1)

            def split_lo(self, dve, ch):
                dve.wait_ge(hi_ready, ch.number + 1)
                a = slice(0, self.size)
                ve.tensor_tensor(w_lo[:, ch.slot, a], raw[:, ch.slot, a], w_hi[:, ch.slot, a].bitcast(F32),
                                 ALU.subtract).then_inc(lo_ready, 1)

            def with_split(self, engine, split, body, steps=None, per_chunk=0):
                def both(ch):
                    if not isinstance(ch.index, int) or ch.index < self.count - LEAD:
                        split(self, engine, ch.ahead(LEAD))
                    elif self.next:
                        split(self.next, engine, Chunk(self.next.first, 0, ch.index + LEAD - self.count))
                    if body:
                        body(ch)
                each_chunk(engine, self.first, self.count, both, steps, per_chunk, keep=LEAD)

            def evac_scalar(self, act, step): return None
            def evac_vector(self, dve, step): return None, 0

            def scalar(self, act, step):
                self.with_split(act, Stream.split_hi, self.evac_scalar(act, step))

            def vector(self, dve, step):
                body, per_chunk = self.evac_vector(dve, step)
                self.with_split(dve, Stream.split_lo, body, step, per_chunk)

        class Setup(Stage):
            def sync(self, sp):
                kept = where["onehot"][0]
                sp.dma_start(const[:], consts[:, 0:kept]).then_inc(const_in, 16)
                sp.dma_start(arena[:, 1024:1024 + 2 * TOEP], consts[:, kept:kept + 2 * TOEP]).then_inc(const_in, 16)
                sp.dma_start(cols[:], W["cols"]).then_inc(const_in, 16)
                sp.dma_start(rowv[:], bass.AP(W["rowv"].tensor, 0, [[0, P], [1, N_ROWV]])).then_inc(const_in, 16)
                sp.dma_start(w_dt[:], W["w_dt"]).then_inc(const_in, 16)
                sp.dma_start(w_kr[:], W["w_kr"]).then_inc(const_in, 16)
                sp.dma_start(resid[:, :, 0:S], W["x"]).then_inc(const_in, 16)
                sp.dma_start(resid[:, :, S:2 * S], W["ctx"]).then_inc(const_in, 16)
                sp.dma_start(small[0:N_BUCKETS, 0:NG * HG], W["rel_bias"]).then_inc(const_in, 16)
                sp.wait_ge(bias_rows, 1)
                sp.dma_start(arena[0:8 * RPB_R, 512 + 48:512 + 48 + RPB_C], W["rpb"]).then_inc(bias_in, 16)
                sp.wait_ge(bias_in, 16)
                sp.dma_start(scratch_rpb, arena[0:8 * RPB_R, 512:512 + RPB_PAD]).then_inc(bias_in, 16)
                sp.wait_ge(bias_rows, 2)
                sp.dma_start(scratch_rel, arena[0:NG * HG, 0:TOEP]).then_inc(bias_in, 16)
                sp.wait_ge(bias_in, 48)

            def tensor(self, pe):
                pe.wait_ge(const_in, 9 * 16)
                te.matmul(psum[0:NG * HG, 0, 0:TOEP], small[0:N_BUCKETS, 0:NG * HG],
                          arena[0:N_BUCKETS, 1024:1024 + TOEP], start=True, stop=True).then_inc(mm, 1)

            def scalar(self, act, step):
                act.wait_ge(const_in, 9 * 16)
                act.wait_ge(chunk_done, CRED)
                for n in range(LEAD):
                    streams[0].split_hi(act, Chunk(0, 0, n))

            def vector(self, dve, step):
                ve.memset(small[:, 760:764], 0.0).then_inc(chunk_done, CRED)
                ve.memset(small[:, 764:768], 0.0).then_inc(chunk_free, CRED)
                ve.memset(small[:, 756:760], 0.0).then_inc(lo_ready, CRED)
                ve.memset(arena[:, 512:512 + RPB_PAD], 0.0).then_inc(bias_rows, 1)
                dve.wait_ge(const_in, 9 * 16)
                dve.wait_ge(mm, self.mm0 + 1)
                ve.tensor_tensor(arena[0:NG * HG, 0:TOEP], psum[0:NG * HG, 0, 0:TOEP],
                                 arena[0:NG * HG, 1024 + TOEP:1024 + 2 * TOEP], ALU.add).then_inc(bias_rows, 1)
                for n in range(LEAD):
                    streams[0].split_lo(dve, Chunk(0, 0, n))

            def __init__(self):
                self.mm0 = take("mm", 1)

        class Modulation(Stream):
            def __init__(self, layer):
                self.layer, self.n = layer, NMOD * D // TW
                self.stream(W["w_mod"][layer * 2 * self.n:(layer + 1) * 2 * self.n], KD // 2, TW, 2 * self.n)
                self.rows_sb = arena[0:2, 0:NMOD * D]
                self.mm0 = take("mm", 1)

            def tensor(self, pe):
                def body(ch):
                    half = ch.j % 2
                    self.begin(pe, ch)
                    for k in range(self.rows):
                        kk = half * self.rows + k
                        last = self.product(psum[0:2, 2 * ((ch.slot - half) % RING), 0:TW], ch,
                                            slice(k * TW, (k + 1) * TW), True, cond[0][:, 2 * kk:2 * kk + 2],
                                            cond[1][:, 2 * kk:2 * kk + 2], kk == 0, kk == KD - 1)
                    last.then_inc(chunk_done, 1)
                each_chunk(pe, self.first, self.count, body)
                pe.wait_ge(chunk_free, CRED + self.first + self.count)
                for m in range(NMOD * KD):
                    last = te.matmul(psum[:, 0, 2 * m:2 * m + 2], self.rows_sb[:, m * P:(m + 1) * P],
                                     ident[0:2, 0:2], start=True, stop=True)
                last.then_inc(mm, 1)

            def evac_scalar(self, act, step):
                def body(ch):
                    if ch.j % 2 == 1:
                        act.wait_ge(chunk_done, CRED + ch.number + 1)
                        se.copy(self.rows_sb[:, bass.ds((ch.index - 1) * P, TW)],
                                psum[0:2, 2 * ((ch.slot - 1) % RING), 0:TW]).then_inc(chunk_free, 2)
                return body

            def vector(self, dve, step):
                super().vector(dve, step)
                dve.wait_ge(mm, self.mm0 + 1)
                nm = NMOD * KD
                mine = mod[:, self.layer * nm:(self.layer + 1) * nm, :]
                bm = col("b_mod", self.layer * nm, nm)
                for side in range(2):
                    step(ve.tensor_tensor(mine[:, :, side], psum[:, 0, side:2 * nm:2], bm, ALU.add))
                for which in (1, 4, 7):
                    a = mine[:, which * KD:(which + 1) * KD, :]
                    ve.tensor_scalar(a, a, 1.0, None, ALU.add)
                for which in (2, 8):
                    a = mine[:, which * KD:(which + 1) * KD, :]
                    ve.tensor_scalar(a, a, 0.5, None, ALU.mult)



        class Conditions(Stage):
            def scalar(self, act, step):
                v = small[:, 32:32 + 2 * KD]
                step(se.activation(v, col("cond", 0, 2 * KD), ACT.Silu))
                se.copy(cond[0][:], v).then_inc(av, 1)

            def __init__(self):
                self.av0 = take("av", 1)

            def vector(self, dve, step):
                dve.wait_ge(av, self.av0 + 1)
                ve.tensor_tensor(cond[1][:], small[:, 32:32 + 2 * KD], cond[0][:].bitcast(F32), ALU.subtract)

        class LinearT(Stream):
            def __init__(self, weights, row_tiles, pairs, x, tiles, dest):
                self.stream(weights, row_tiles // 2, TW, 2 * pairs)
                self.x, self.tiles, self.dest = x, tiles, dest

            def tensor(self, pe):
                def body(ch):
                    half = ch.j % 2
                    self.begin(pe, ch)
                    if half == 0:
                        pe.wait_ge(chunk_free, ch.number + 2)
                    bank = 2 * ((ch.slot - half) % RING)
                    for t in range(self.tiles):
                        for k in range(self.rows):
                            kk = half * self.rows + k
                            last = self.product(psum[:, bank + t, 0:TW], ch, slice(k * TW, (k + 1) * TW), True,
                                                self.x[0][:, kk, t * P:(t + 1) * P],
                                                self.x[1][:, kk, t * P:(t + 1) * P],
                                                kk == 0, kk == 2 * self.rows - 1)
                    last.then_inc(chunk_done, 1)
                each_chunk(pe, self.first, self.count, body)

            def evac_scalar(self, act, step):
                def body(ch):
                    if ch.j % 2 == 1:
                        act.wait_ge(chunk_done, CRED + ch.number + 1)
                        bank = 2 * ((ch.slot - 1) % RING)
                        se.copy(self.dest[:, 0:self.tiles, bass.ds((ch.index - 1) * P, TW)],
                                psum[:, bank:bank + self.tiles, 0:TW]).then_inc(chunk_free, 2)
                return body

        class LinearF(Stream):
            def __init__(self, weights, rows, count, x, tokens, dest, func=ACT.Copy):
                self.stream(weights, rows, FW, count)
                self.x, self.tokens, self.dest, self.func = x, tokens, dest, func

            def tensor(self, pe):
                def body(ch):
                    self.begin(pe, ch)
                    for k in range(self.rows):
                        last = self.product(psum[:, ch.bank, 0:self.tokens], ch, slice(k * FW, (k + 1) * FW), False,
                                            self.x[0][:, k, 0:self.tokens], self.x[1][:, k, 0:self.tokens],
                                            k == 0, k == self.rows - 1)
                    last.then_inc(chunk_done, 1)
                each_chunk(pe, self.first, self.count, body)

            def evac_scalar(self, act, step):
                def body(ch):
                    act.wait_ge(chunk_done, CRED + ch.number + 1)
                    se.activation(pick(self.dest, ch.index), psum[:, ch.bank, 0:self.tokens], self.func
                                  ).then_inc(chunk_free, 1)
                return body

        class IntoResid(LinearF):
            def __init__(self, weights, rows, x, tokens, gate):
                super().__init__(weights, rows, KD, x, tokens, None)
                self.gate = gate

            def evac_scalar(self, act, step):
                return None

            def evac_vector(self, dve, step):
                def body(ch):
                    dve.wait_ge(chunk_done, CRED + ch.number + 1)
                    if self.gate is None:
                        r = pick(resid[:, :, 0:self.tokens], ch.index)
                        last = ve.tensor_tensor(r, r, psum[:, ch.bank, 0:self.tokens], ALU.add)
                    else:
                        base = (self.gate[0] * NMOD + self.gate[1]) * KD
                        for side in range(self.tokens // S):
                            a = slice(side * S, (side + 1) * S)
                            r = pick(resid[:, :, a], ch.index)
                            last = ve.scalar_tensor_tensor(
                                out=r, in0=psum[:, ch.bank, a], scalar=pick(mod[:, base:base + KD, side:side + 1],
                                                                            ch.index),
                                in1=r, op0=ALU.mult, op1=ALU.add)
                    last.then_inc(chunk_free, 1)
                return body, 0

        class Norm(Stage):
            def __init__(self, tokens, gain, shift, in_place=False):
                self.tokens, self.gain, self.shift, self.in_place = tokens, gain, shift, in_place
                self.mm0, self.vv0, self.av0 = take("mm", 1), take("vv", 1 + KD), take(
                    "av", (1 if in_place else 2) * KD + 1)

            def tensor(self, pe):
                for k in range(KD):
                    pe.wait_ge(av, self.av0 + k + 1)
                    last = te.matmul(psum[:, 0, 0:self.tokens], ones, norm_sq[:, k, 0:self.tokens],
                                     start=(k == 0), stop=(k == KD - 1))
                last.then_inc(mm, 1)

            def scalar(self, act, step):
                w = self.tokens
                for k in range(KD):
                    se.activation(norm_sq[:, k, 0:w], resid[:, k, 0:w], ACT.Square).then_inc(av, 1)
                act.wait_ge(vv, self.vv0 + 1)
                step(se.activation(rstd[:, 0:w], rstd[:, 0:w], ACT.Ln))
                se.activation(rstd[:, 0:w], rstd[:, 0:w], ACT.Exp, scale=-0.5).then_inc(av, 1)
                if self.in_place:
                    return
                for k in range(KD):
                    act.wait_ge(vv, self.vv0 + 2 + k)
                    if self.shift is None:
                        last = se.copy(normed[0][:, k, 0:w], norm_tmp[:, k, 0:w])
                    else:
                        for side in range(w // S):
                            a = slice(side * S, (side + 1) * S)
                            last = se.activation(normed[0][:, k, a], norm_tmp[:, k, a], ACT.Identity,
                                                 bias=self.shift(k, side))
                    last.then_inc(av, 1)

            def vector(self, dve, step):
                w = self.tokens
                dve.wait_ge(mm, self.mm0 + 1)
                ve.tensor_scalar(rstd[:, 0:w], psum[:, 0, 0:w], 1.0 / D, EPS, ALU.mult, ALU.add).then_inc(vv, 1)
                dve.wait_ge(av, self.av0 + KD + 1)
                out = resid if self.in_place else norm_tmp
                for k in range(KD + 1):
                    if k < KD:
                        for side in range(w // S):
                            a = slice(side * S, (side + 1) * S)
                            last = ve.scalar_tensor_tensor(out=out[:, k, a], in0=resid[:, k, a],
                                                           scalar=self.gain(k, side), in1=rstd[:, a],
                                                           op0=ALU.mult, op1=ALU.mult)
                        last.then_inc(vv, 1)
                    if k >= 1 and not self.in_place:
                        dve.wait_ge(av, self.av0 + KD + 1 + k)
                        hi, lo = (normed[n][:, k - 1, 0:w] for n in range(2))
                        if self.shift is None:
                            ve.tensor_tensor(lo, norm_tmp[:, k - 1, 0:w], hi.bitcast(F32), ALU.subtract)
                        else:
                            for side in range(w // S):
                                a = slice(side * S, (side + 1) * S)
                                ve.scalar_tensor_tensor(out=lo[:, a], in0=norm_tmp[:, k - 1, a],
                                                        scalar=self.shift(k - 1, side), in1=hi[:, a].bitcast(F32),
                                                        op0=ALU.add, op1=ALU.subtract)

        def modulated(layer, shift, scale, tokens):
            return Norm(tokens, lambda k, s: mod[:, (layer * NMOD + scale) * KD + k, s:s + 1],
                        lambda k, s: mod[:, (layer * NMOD + shift) * KD + k, s:s + 1])

        class FfnUp(LinearF):
            def __init__(self, weights, half, tokens):
                super().__init__(weights[half * KF:(half + 1) * KF], KD, KF, normed, tokens, None)
                self.av0, self.vv0 = take("av", self.count), take("vv", self.count)

            def evac_scalar(self, act, step):
                n = self.tokens

                def body(ch):
                    t = ch.j // 2
                    if ch.j % 2 == 0:
                        act.wait_ge(chunk_done, CRED + ch.number + 1)
                        act.wait_ge(chunk_free, CRED + ch.number - 2)
                        se.activation(ffn_tmp[:, t, 0, 0:n], psum[:, ch.bank, 0:n], ACT.Silu).then_inc(av, 1)
                    else:
                        act.wait_ge(vv, self.vv0 + ch.index + 1)
                        se.copy(pick(hidden[0][:, :, 0:n], hidden_tile(ch)), ffn_tmp[:, t, 1, 0:n]).then_inc(av, 1)
                return body

            def evac_vector(self, dve, step):
                n = self.tokens

                def body(ch):
                    t = ch.j // 2
                    if ch.j % 2 == 1:
                        dve.wait_ge(av, self.av0 + ch.index)
                        dve.wait_ge(chunk_done, CRED + ch.number + 1)
                        ve.tensor_tensor(ffn_tmp[:, t, 1, 0:n], ffn_tmp[:, t, 0, 0:n],
                                         psum[:, ch.bank, 0:n], ALU.mult).then_inc(vv, 2)
                        dve.wait_ge(av, self.av0 + ch.index + 1)
                        tile = hidden_tile(ch)
                        ve.tensor_tensor(pick(hidden[1][:, :, 0:n], tile), ffn_tmp[:, t, 1, 0:n],
                                         pick(hidden[0][:, :, 0:n], tile).bitcast(F32), ALU.subtract
                                         ).then_inc(chunk_free, 2)
                return body, 0

        def hidden_tile(ch):
            return ch.half_index


        class Map:
            def __init__(self, scores, biases, sink=None):
                self.scores, self.biases, self.sink = scores, biases, sink
                self.width = sum(n for n, _ in biases)

        class Unit:
            def __init__(self, maps, values, out, scale, lam=None):
                self.maps, self.values, self.out, self.scale, self.lam = maps, values, out, scale, lam

        class Attention(Stage):
            def __init__(self, units, space):
                self.units = units
                self.base = take("units", len(units))
                w = max(max(sum(m.width for m in u.maps), 128) for u in units)
                self.s = space[:, 0:2 * w].rearrange("p (b n) -> p b n", b=2)
                tiles = max(len(u.values) for u in units)
                self.turned = space[:, 2 * w:2 * w + tiles * P]
                self.stat = small[:, 128:128 + 32].rearrange("p (b n) -> p b n", b=2)

            def tensor(self, pe):
                for u in range(len(self.units) + 1):
                    if u < len(self.units):
                        unit, b = self.units[u], self.base + u
                        if u >= 2:
                            pe.wait_ge(at_read, b - 1)
                        for n, m in enumerate(unit.maps):
                            at = 0
                            for q, keys in m.scores:
                                width = keys.shape[1]
                                bank, off = divmod((2 * (u % 2) + n) * 512 + at, 512)
                                last = te.matmul(psum[:, bank, off:off + width], q, keys, start=True, stop=True)
                                at += width
                        last.then_inc(at_scores, 1)
                    if u >= 1:
                        unit, b = self.units[u - 1], self.base + u - 1
                        pe.wait_ge(at_probs, b + 1)
                        probs = self.s[:, (u - 1) % 2, :]
                        for j in range(len(unit.values)):
                            last = te.transpose(psum[:, 4 + j // 4, (j % 4) * P:(j % 4 + 1) * P],
                                                probs[:, j * P:(j + 1) * P], ident)
                        last.then_inc(at_turned, 1)
                        pe.wait_ge(at_copied, b + 1)
                        if u - 1 >= 2:
                            pe.wait_ge(at_out, b - 1)
                        for j, v in enumerate(unit.values):
                            last = te.matmul(psum[0:v.shape[1], 6 + (u - 1) % 2, 0:P], v,
                                             self.turned[:, j * P:(j + 1) * P],
                                             start=(j == 0), stop=(j == len(unit.values) - 1))
                        last.then_inc(at_pv, 1)

            def scalar(self, act, step):
                for u in range(len(self.units) + 1):
                    if u < len(self.units):
                        unit, b = self.units[u], self.base + u
                        act.wait_ge(at_max, b + 1)
                        at, stat = 0, self.stat[:, u % 2, :]
                        for n, m in enumerate(unit.maps):
                            a = self.s[:, u % 2, at:at + m.width]
                            last = se.activation(a, a, ACT.Exp, bias=stat[:, n:n + 1], accum_out=stat[:, 4 + n:5 + n])
                            if m.sink is not None:
                                last = se.activation(stat[:, 8 + n:9 + n], m.sink, ACT.Exp, bias=stat[:, n:n + 1])
                            at += m.width
                        last.then_inc(at_exp, 1)
                    if u >= 1:
                        unit, b = self.units[u - 1], self.base + u - 1
                        act.wait_ge(at_turned, b + 1)
                        n = len(unit.values) * P
                        se.copy(self.turned[:, 0:n], psum[:, 4:6, :].rearrange("p b n -> p (b n)")[:, 0:n]
                                ).then_inc(at_copied, 1)

            def vector(self, dve, step):
                flat = psum[:].rearrange("p b n -> p (b n)")
                for u in range(len(self.units) + 2):
                    if u >= 2:
                        unit, b = self.units[u - 2], self.base + u - 2
                        dve.wait_ge(at_pv, b + 1)
                        if len(unit.out) == 1:
                            ve.tensor_copy(unit.out[0], psum[0:unit.out[0].shape[0], 6 + u % 2, 0:P]).then_inc(at_out, 1)
                        else:
                            hi, lo = unit.out
                            src = psum[0:hi.shape[0], 6 + u % 2, 0:P]
                            step(ve.tensor_copy(hi, src))
                            ve.tensor_tensor(lo, src, hi.bitcast(F32), ALU.subtract).then_inc(at_out, 1)
                    if u < len(self.units):
                        unit, b = self.units[u], self.base + u
                        dve.wait_ge(at_scores, b + 1)
                        at, stat = 0, self.stat[:, u % 2, :]
                        for n, m in enumerate(unit.maps):
                            inner = 0
                            for width, bias in m.biases:
                                off = (2 * (u % 2) + n) * 512 + inner
                                src, dst = flat[:, off:off + width], self.s[:, u % 2, at:at + width]
                                if bias is not None and len(bias.shape) == 3:
                                    src, dst = (a.rearrange("p (g n) -> p g n", g=bias.shape[1]) for a in (src, dst))
                                if bias is None:
                                    last = ve.tensor_scalar(dst, src, unit.scale, None, ALU.mult)
                                else:
                                    last = ve.scalar_tensor_tensor(out=dst, in0=src, scalar=unit.scale, in1=bias,
                                                                   op0=ALU.mult, op1=ALU.add)
                                at, inner = at + width, inner + width
                        last.then_inc(at_read, 1)
                        dve.wait_ge(at_read, b + 1)
                        at = 0
                        for n, m in enumerate(unit.maps):
                            last = ve.tensor_reduce(stat[:, n:n + 1], self.s[:, u % 2, at:at + m.width], AX.X, ALU.max,
                                                    negate=True)
                            at += m.width
                            if m.sink is not None:
                                step(last)
                                last = ve.scalar_tensor_tensor(out=stat[:, n:n + 1], in0=m.sink, scalar=-1.0,
                                                               in1=stat[:, n:n + 1], op0=ALU.mult, op1=ALU.min)
                        last.then_inc(at_max, 1)
                    if 1 <= u <= len(self.units):
                        unit, b = self.units[u - 1], self.base + u - 1
                        dve.wait_ge(at_exp, b + 1)
                        stat, s = self.stat[:, (u - 1) % 2, :], self.s[:, (u - 1) % 2, :]
                        k = len(unit.maps)
                        if unit.maps[0].sink is not None:
                            step(ve.tensor_tensor(stat[:, 4:5], stat[:, 4:5], stat[:, 8:9], ALU.add))
                        step(ve.reciprocal(stat[:, 4:4 + k], stat[:, 4:4 + k]))
                        w = unit.maps[0].width
                        if k == 1:
                            last = ve.tensor_scalar(s[:, 0:w], s[:, 0:w], stat[:, 4:5], None, ALU.mult)
                        else:
                            step(ve.tensor_tensor(stat[:, 5:6], stat[:, 5:6], unit.lam, ALU.mult))
                            step(ve.tensor_scalar(s[:, w:2 * w], s[:, w:2 * w], stat[:, 5:6], None, ALU.mult))
                            last = ve.scalar_tensor_tensor(out=s[:, 0:w], in0=s[:, 0:w], scalar=stat[:, 4:5],
                                                           in1=s[:, w:2 * w], op0=ALU.mult, op1=ALU.subtract)
                        last.then_inc(at_probs, 1)


        def both(pair, *index):
            return [t[index] for t in pair]

        attn1 = split_at("attn1", (0, 4 * S), 4, S)
        qk1 = at(2048, 24, S)
        v1 = at(8192, NT, AW)
        relbias = at(11264, NG * HG, 2, P)
        space1 = arena[:, 17408:19712]

        class Mirror(Stage):
            def __init__(self, flat, mirror, loads, mask=None):
                self.flat, self.mirror, self.loads, self.mask = flat, mirror, loads, mask
                self.n = flat.shape[1] // 512
                self.mm0, self.vv0 = take("mm", self.n), take("vv", self.n)
                self.landed = take("bias", 16 * len(loads)) + 16 * len(loads)

            def scalar(self, act, step):
                for dst, src in self.loads:
                    act.dma_start(dst, src).then_inc(bias_in, 16)

            def tensor(self, pe):
                pe.wait_ge(bias_in, self.landed)
                for b in range(self.n):
                    if b >= 8:
                        pe.wait_ge(vv, self.vv0 + b - 7)
                    te.matmul(psum[:, b % 8, :], self.mirror, self.flat[:, b * 512:(b + 1) * 512],
                              start=True, stop=True).then_inc(mm, 1)

            def vector(self, dve, step):
                for b in range(self.n):
                    dve.wait_ge(mm, self.mm0 + b + 1)
                    dst = self.flat[:, b * 512:(b + 1) * 512]
                    if self.mask is None:
                        ve.tensor_copy(dst, psum[:, b % 8, :]).then_inc(vv, 1)
                    else:
                        dst, src = (a.rearrange("p (r n) -> p r n", n=S) for a in (dst, psum[:, b % 8, :]))
                        ve.tensor_tensor(dst, src, self.mask.rearrange("p (o n) -> p o n", o=1).to_broadcast(
                            [P, 512 // S, S]), ALU.add).then_inc(vv, 1)

        def relative_bias():
            loads = [(relbias[:, :, s, :], bass.AP(scratch_rel.tensor, P * s, [[1, P], [TOEP, NG * HG], [1, P]]))
                     for s in range(2)]
            return Mirror(relbias.rearrange("p h s j -> p (h s j)"), C("mirror"), loads)

        def attention1_units():
            units = []
            for t in range(NT):
                for h in range(HG):
                    a = slice((h % 2) * HD, (h % 2 + 1) * HD)
                    scores, values = [], []
                    for g in range(NG):
                        tile = g * 4 + h // 2
                        scores.append((qk1[a, tile, t * P:(t + 1) * P], qk1[a, 12 + tile, 0:(t + 1) * P]))
                        values += [v1[:, kt, (g * HG + h) * HD:(g * HG + h + 1) * HD] for kt in range(t + 1)]
                    bias = relbias[:, h::HG, 1 - t:2, :].rearrange("p g s j -> p g (s j)")
                    units.append(Unit([Map(scores, [(NG * (t + 1) * P, bias)])], values,
                                      both(attn1, a, h // 2, slice(t * P, (t + 1) * P)), HD ** -0.5))
            return units

        xbc = at(2048, KX, S + CONV - 1)
        z1 = at(8264, NT, DI)
        conv = at(12360, KX, S)
        x_tok = at(2048, NT, DI)
        gates1 = at(12360, 2 * KD, S)
        xdt = at(16456, NT, DI)
        cb = at(6144, SG, 384)
        y_square = arena[:, 7680:7680 + GW]
        decay = at(20552, 2, 384)
        ssm_t = split_at("ssm_t", (8264, 16456), KI, S)
        merged = split_at("merged", (2048, 4096), KD, S)
        branch_tmp = at(6144, 2, S)
        dt_x = [n[:].bitcast(F32) for n in normed]
        dt = small[:, 256:256 + NT * SH]
        neg_la = small[:, 320:320 + NT * SH]
        dta = small[:, 384:384 + NT * SH]
        a_exp = small[:, 448:448 + SH]
        ssq = small[:, 480:480 + NT * SG]
        dt_tmp = small[:, 512:512 + NT * SH]

        class Only(Stage):
            def __init__(self, engine, program):
                setter = {"tensor": 0, "scalar": 1, "vector": 2}[engine]
                self.which, self.program = setter, program

            def tensor(self, pe):
                if self.which == 0:
                    self.program()

            def scalar(self, act, step):
                if self.which == 1:
                    self.program(step)

            def vector(self, dve, step):
                if self.which == 2:
                    self.program(step)

        class ConvX(LinearF):
            def __init__(self):
                super().__init__(W["w_x"], KD, KX, normed, S, xbc[:, :, CONV - 1:])
                self.vv0 = take("vv", 1)

            def scalar(self, act, step):
                act.wait_ge(vv, self.vv0 + 1)
                super().scalar(act, step)

            def vector(self, dve, step):
                ve.memset(xbc[:, :, 0:CONV - 1], 0.0).then_inc(vv, 1)
                dve.wait_ge(vv, self.vv0 + 1)
                super().vector(dve, step)

            def evac_vector(self, dve, step):
                conv_w = [col("conv_w", w * KX, KX).rearrange("p (k o) -> p k o", o=1) for w in range(CONV)]
                conv_b = col("conv_b", 0, KX).rearrange("p (k o) -> p k o", o=1)

                def body(ch):
                    dve.wait_ge(chunk_free, CRED + ch.number + 1)
                    y = pick(conv, ch.index)
                    for w in range(CONV):
                        x_w = pick(xbc[:, :, w:w + S], ch.index)
                        if w == 0:
                            step(ve.tensor_scalar(y, x_w, pick(conv_w[0], ch.index), pick(conv_b, ch.index),
                                                  ALU.mult, ALU.add))
                        else:
                            step(ve.scalar_tensor_tensor(out=y, in0=x_w, scalar=pick(conv_w[w], ch.index), in1=y,
                                                         op0=ALU.mult, op1=ALU.add))
                return body, CONV

        class Turn(Stage):
            def __init__(self, tiles, evac, lo=None):
                self.tiles, self.evac, self.lo, self.each = tiles, evac, lo, 4
                self.banks = -(-len(tiles) // self.each)
                self.mm0, self.av0 = take("mm", self.banks), take("av", self.banks)

            def tensor(self, pe):
                for n, tile in enumerate(self.tiles):
                    k = tile.shape[1]
                    last = te.transpose(psum[0:k, n // self.each, (n % self.each) * P:(n % self.each + 1) * P],
                                        tile, ident)
                    if n % self.each == self.each - 1 or n == len(self.tiles) - 1:
                        last.then_inc(mm, 1)

            def scalar(self, act, step):
                for b in range(self.banks):
                    act.wait_ge(mm, self.mm0 + b + 1)
                    self.evac(b).then_inc(av, 1)

            def vector(self, dve, step):
                if self.lo:
                    for b in range(self.banks):
                        dve.wait_ge(av, self.av0 + b + 1)
                        self.lo(b)

        def silu_conv(step):
            se.activation(conv, conv, ACT.Silu)

        def silu_z(step):
            se.activation(z1, z1, ACT.Silu)

        def dt_projection():
            for t in range(NT):
                for k in range(KD):
                    for n in range(2):
                        te.matmul(psum[:, 0, t * SH:(t + 1) * SH], dt_x[n][:, k, t * P:(t + 1) * P], w_dt[:, k, :],
                                  start=(k == 0 and n == 0), stop=(k == KD - 1 and n == 1))

        def dt_bias(step):
            for t in range(NT):
                a = slice(t * SH, (t + 1) * SH)
                step(ve.tensor_tensor(dt[:, a], psum[:, 0, a], row("dt_bias"), ALU.add))
            step(ve.scalar_tensor_tensor(out=dt_tmp, in0=dt, scalar=-1.0, in1=dt, op0=ALU.mult, op1=ALU.min))
            step(ve.tensor_scalar(dt, dt, 0.0, None, ALU.max))

        def dt_softplus(step):
            se.activation(a_exp, row("a_log"), ACT.Exp)
            step(se.activation(dt_tmp, dt_tmp, ACT.Exp))
            se.activation(dt_tmp, dt_tmp, ACT.Ln, bias=1.0)

        def dt_decay(step):
            step(ve.tensor_tensor(dt, dt, dt_tmp, ALU.add))
            for t in range(NT):
                a = slice(t * SH, (t + 1) * SH)
                ve.scalar_tensor_tensor(out=dta[:, a], in0=dt[:, a], scalar=-1.0, in1=a_exp,
                                        op0=ALU.mult, op1=ALU.mult)

        def sum_decay():
            upper = C("upper")[:, 0:P]
            te.matmul(psum[:, 0, 0:SH], upper, dta[:, 0:SH], start=True, stop=True)
            te.matmul(psum[:, 0, SH:2 * SH], ones, dta[:, 0:SH], start=True, stop=False)
            te.matmul(psum[:, 0, SH:2 * SH], upper, dta[:, SH:2 * SH], start=False, stop=True)

        def negate_sums(step):
            ve.tensor_scalar(neg_la, psum[:, 0, 0:2 * SH], -1.0, None, ALU.mult)

        def heads_of(ap):
            return ap.rearrange("p (h d) -> p h d", d=64)

        def per_head(v):
            return v.rearrange("p (h o) -> p h o", o=1).to_broadcast([P, SH, 64])

        def scale_x(step):
            for t in range(NT):
                ve.tensor_tensor(heads_of(xdt[:, t, :]), heads_of(x_tok[:, t, :]),
                                 per_head(dt[:, t * SH:(t + 1) * SH]), ALU.mult)
            for t in range(NT):
                a = heads_of(x_tok[:, t, :])
                ve.tensor_tensor(a, a, per_head(row("d_skip")), ALU.mult)

        def cb_products():
            for g in range(SG):
                for t in range(NT):
                    te.matmul(psum[:, g, t * S:t * S + S - t * P], conv[:, KI + g, t * P:(t + 1) * P],
                              conv[:, KI + SG + g, t * P:S], start=True, stop=True)

        def copy_cb(step):
            for g in range(SG):
                se.copy(cb[:, g, :], psum[:, g, 0:384])

        class Scan(Stage):
            def tensor(self, pe):
                upper = C("upper")
                for h in range(SH + 1):
                    if h < SH:
                        if h >= 2:
                            pe.wait_ge(scan_read, h - 1)
                        te.matmul(psum[:, h % 2, 0:S], dta[:, h:h + 1].to_broadcast([P, P]), upper,
                                  start=True, stop=False)
                        te.matmul(psum[:, h % 2, P:S], dta[:, SH + h:SH + h + 1].to_broadcast([P, P]), upper[:, 0:P],
                                  start=False, stop=True).then_inc(scan_sums, 1)
                    if h >= 1:
                        i = h - 1
                        g = i // SHG
                        pe.wait_ge(scan_masked, i + 1)
                        if i % SHG == 0 and g >= 2:
                            pe.wait_ge(scan_gated, g - 1)
                        m, bank, a = decay[:, i % 2, :], 4 + 2 * (g % 2), slice((i % SHG) * 64, (i % SHG + 1) * 64)
                        xa = slice(i * 64, (i + 1) * 64)
                        te.matmul(psum[:, bank, a], m[:, 0:P], xdt[:, 0, xa], start=True, stop=True)
                        te.matmul(psum[:, bank + 1, a], m[:, P:S], xdt[:, 0, xa], start=True, stop=False)
                        te.matmul(psum[:, bank + 1, a], m[:, S:384], xdt[:, 1, xa], start=False, stop=True
                                  ).then_inc(scan_y, 1)

            def scalar(self, act, step):
                for h in range(SH):
                    act.wait_ge(scan_read, h + 1)
                    se.activation(decay[:, h % 2, :], decay[:, h % 2, :], ACT.Exp).then_inc(scan_exp, 1)

            def vector(self, dve, step):
                causal = C("causal")
                for h in range(SH + 1):
                    if h < SH:
                        dve.wait_ge(scan_sums, h + 1)
                        if h >= 2:
                            dve.wait_ge(scan_y, h - 1)
                        d = decay[:, h % 2, :]
                        ve.scalar_tensor_tensor(out=d[:, 0:S], in0=psum[:, h % 2, 0:S], scalar=neg_la[:, h:h + 1],
                                                in1=causal, op0=ALU.add, op1=ALU.add)
                        ve.scalar_tensor_tensor(out=d[:, S:384], in0=psum[:, h % 2, P:S],
                                                scalar=neg_la[:, SH + h:SH + h + 1], in1=causal[:, 0:P],
                                                op0=ALU.add, op1=ALU.add).then_inc(scan_read, 1)
                    if h >= 1:
                        i = h - 1
                        dve.wait_ge(scan_exp, i + 1)
                        d = decay[:, i % 2, :]
                        ve.tensor_tensor(d, d, cb[:, i // SHG, :], ALU.mult).then_inc(scan_masked, 1)
                        if i % SHG == SHG - 1:
                            g = i // SHG
                            dve.wait_ge(scan_y, i + 1)
                            for t in range(NT):
                                a = slice(g * GW, (g + 1) * GW)
                                y = x_tok[:, t, a]
                                ins = ve.tensor_tensor(y, psum[:, 4 + 2 * (g % 2) + t, :], y, ALU.add)
                                if t == NT - 1:
                                    ins.then_inc(scan_gated, 1)
                                    dve.wait_ge(scan_gated, g + 1)
                                else:
                                    step(ins)
                                step(ve.tensor_tensor(y, y, z1[:, t, a], ALU.mult))
                                n = t * SG + g
                                ve.scalar_tensor_tensor(out=y_square, in0=y, scalar=1.0, in1=y,
                                                        op0=ALU.mult, op1=ALU.mult, accum_out=ssq[:, n:n + 1])

        def mean_square(step):
            ve.tensor_scalar(ssq, ssq, 1.0 / GW, EPS, ALU.mult, ALU.add)

        def inverse_root(step):
            step(se.activation(ssq, ssq, ACT.Ln))
            se.activation(ssq, ssq, ACT.Exp, scale=-0.5)

        def normalise_groups(step):
            for t in range(NT):
                for g in range(SG):
                    y = x_tok[:, t, g * GW:(g + 1) * GW]
                    ve.tensor_scalar(y, y, ssq[:, t * SG + g:t * SG + g + 1], None, ALU.mult)

        def ssm_turned(b):
            for m in range(2):
                last = se.activation(ssm_t[0][:, 2 * b + m, :], psum[:, b, m * S:(m + 1) * S], ACT.Copy,
                                     scale=col("ssm_norm", 2 * b + m))
            return last

        def ssm_turned_lo(b):
            for m in range(2):
                last = ve.scalar_tensor_tensor(out=ssm_t[1][:, 2 * b + m, :], in0=psum[:, b, m * S:(m + 1) * S],
                                               scalar=col("ssm_norm", 2 * b + m),
                                               in1=ssm_t[0][:, 2 * b + m, :].bitcast(F32),
                                               op0=ALU.mult, op1=ALU.subtract)
            return last

        class Branches(Stream):
            def __init__(self):
                self.stream(W["w_branch"], 10, FW, 2 * KD)
                self.av0, self.vv0 = take("av", 2 * KD), take("vv", 2 * KD)

            def tensor(self, pe):
                def body(ch):
                    self.begin(pe, ch)
                    half = ch.j % 2
                    bank = 2 * ((ch.slot - half) % RING)
                    for k in range(10):
                        tile = half * 10 + k
                        x, m = (attn1, tile) if tile < 4 else (ssm_t, tile - 4)
                        last = self.product(psum[:, bank + (tile >= 4), 0:S], ch, slice(k * FW, (k + 1) * FW), False,
                                            x[0][:, m, :], x[1][:, m, :], tile in (0, 4), tile in (3, 19))
                    last.then_inc(chunk_done, 1)
                each_chunk(pe, self.first, self.count, body)

            def evac_scalar(self, act, step):
                def body(ch):
                    if ch.j % 2 == 1:
                        act.wait_ge(vv, self.vv0 + ch.index + 1)
                        se.copy(pick(merged[0], ch.half_index), branch_tmp[:, 0, :]).then_inc(av, 2)
                return body

            def evac_vector(self, dve, step):
                def body(ch):
                    if ch.j % 2 == 0:
                        return
                    bank = 2 * ((ch.slot - 1) % RING)
                    dve.wait_ge(chunk_done, CRED + ch.number + 1)
                    dve.wait_ge(chunk_free, CRED + ch.number - 1)
                    a, b = branch_tmp[:, 0, :], branch_tmp[:, 1, :]
                    step(ve.tensor_tensor(a, psum[:, bank, 0:S], pick(gates1, ch.half_index), ALU.mult))
                    step(ve.tensor_tensor(b, psum[:, bank + 1, 0:S], pick(gates1[:, KD:], ch.half_index), ALU.mult))
                    ve.tensor_tensor(a, a, b, ALU.add).then_inc(vv, 2)
                    dve.wait_ge(av, self.av0 + ch.index + 1)
                    ve.tensor_tensor(pick(merged[1], ch.half_index), a, pick(merged[0], ch.half_index).bitcast(F32),
                                     ALU.subtract).then_inc(chunk_free, 2)
                return body, 1


        TT = 2 * NT

        class HeadNorm(Stage):
            def __init__(self, items, space):
                self.items = items
                self.av0, self.vv0 = take("av", len(items) + 1), take("vv", 1)
                self.squares, self.stats, at, st = [], [], 0, 576
                for _, tiles, heads, width, *_ in items:
                    self.squares.append(space[:, at:at + tiles * heads * width])
                    self.stats.append(small[:, st:st + tiles * heads])
                    at, st = at + tiles * heads * width, st + tiles * heads
                assert st <= 760 and at <= space.shape[1]
                self.all_stats = small[:, 576:st]

            def scalar(self, act, step):
                for (view, tiles, heads, width, *_), sq in zip(self.items, self.squares):
                    for t in range(tiles):
                        last = se.activation(sq[:, t * heads * width:(t + 1) * heads * width].rearrange(
                            "p (h d) -> p h d", h=heads), view(t), ACT.Square)
                    last.then_inc(av, 1)
                act.wait_ge(vv, self.vv0 + 1)
                step(se.activation(self.all_stats, self.all_stats, ACT.Ln))
                se.activation(self.all_stats, self.all_stats, ACT.Exp, scale=-0.5).then_inc(av, 1)

            def vector(self, dve, step):
                for n, ((_, tiles, heads, width, *_), sq, st) in enumerate(zip(self.items, self.squares, self.stats)):
                    dve.wait_ge(av, self.av0 + n + 1)
                    step(ve.tensor_reduce(st, sq.rearrange("p (h d) -> p h d", d=width), AX.X, ALU.add))
                    ins = ve.tensor_scalar(st, st, 1.0 / width, EPS, ALU.mult, ALU.add)
                    step(ins)
                ve.tensor_copy(self.all_stats, self.all_stats).then_inc(vv, 1)
                dve.wait_ge(av, self.av0 + len(self.items) + 1)
                for n, ((view, tiles, heads, width, gain, rope, out), sq, st) in enumerate(
                        zip(self.items, self.squares, self.stats)):
                    for t in range(tiles):
                        shape = [P, heads, width]
                        r = st[:, t * heads:(t + 1) * heads].rearrange("p (h o) -> p h o", o=1).to_broadcast(shape)
                        if gain is None:
                            ve.tensor_tensor(out(t), view(t), r, ALU.mult)
                            continue
                        g = gain.rearrange("p (o d) -> p o d", o=1).to_broadcast(shape)
                        if rope is None or t >= NT:
                            step(ve.tensor_tensor(view(t), view(t), r, ALU.mult))
                            ve.tensor_tensor(out(t), view(t), g, ALU.mult)
                            continue
                        step(ve.tensor_tensor(view(t), view(t), r, ALU.mult))
                        step(ve.tensor_tensor(view(t), view(t), g, ALU.mult))
                        cos, sin = (C(name)[:, t * width:(t + 1) * width] for name in rope)
                        q = width // 4
                        rot = sq[:, t * heads * width:(t + 1) * heads * width].rearrange("p (h d) -> p h d", h=heads)
                        for axis in range(2):
                            for half in range(2):
                                a, b = (2 * axis + half) * q, (2 * axis + 1 - half) * q
                                s = sin[:, a:a + q].rearrange("p (o d) -> p o d", o=1).to_broadcast([P, heads, q])
                                ins = ve.tensor_tensor(rot[:, :, a:a + q], view(t)[:, :, b:b + q], s, ALU.mult)
                        step(ins)
                        c = cos.rearrange("p (o d) -> p o d", o=1).to_broadcast(shape)
                        step(ve.tensor_tensor(view(t), view(t), c, ALU.mult))
                        ve.tensor_tensor(out(t), view(t), rot, ALU.add)

        def heads_view(a, start, heads, width, pitch=None, off=0):
            pitch = pitch or width
            return lambda t: a[:, t, start:start + heads * pitch].rearrange(
                "p (h d) -> p h d", d=pitch)[:, :, off:off + width]

        AQ, BQ, AK, AV, BK, BV = 0, 512, 1024, 1152, 1280, 1792
        ab = at(0, TT, 2304)
        q2 = at(9216, 8, 512)
        k2 = at(13312, 5, 512)
        space_ab = arena[:, 15872:15872 + 2560]
        y_b = at(18432, 4, 512)
        lam = small[:, 104:105]
        lam_tmp = small[:, 106:108]
        lam_prod = arena[:, 15872:15872 + HD]
        rope64, rope32 = ("cos64", "sin64"), ("cos32", "sin32")

        def lambda_dots(step):
            for n, (a, b) in enumerate((("lq1", "lk1"), ("lq2", "lk2"))):
                step(ve.tensor_tensor(lam_prod, row(a), row(b), ALU.mult))
                step(ve.tensor_reduce(lam_tmp[:, n:n + 1], lam_prod, AX.X, ALU.add))

        def lambda_exp(step):
            se.activation(lam_tmp, lam_tmp, ACT.Exp)

        def lambda_sum(step):
            step(ve.tensor_tensor(lam, lam_tmp[:, 0:1], lam_tmp[:, 1:2], ALU.subtract))
            step(ve.tensor_scalar(lam, lam, 0.8 - 0.6, None, ALU.add))

        def ab_units():
            units = []
            for t in range(TT):
                ctx_only = t >= NT
                keys = slice(S, 2 * S) if ctx_only else slice(0, 2 * S)
                key_tiles = range(NT, TT) if ctx_only else range(TT)
                for h in range(8):
                    side, pair = h // 4, h % 4
                    a = slice(side * HD, (side + 1) * HD)
                    biases = [(S, None)] if ctx_only else [(S, C("window")[:, t * S:(t + 1) * S]), (S, None)]
                    m = Map([(q2[a, pair, t * P:(t + 1) * P], k2[a, 0, keys])], biases, row("sink")[:, h:h + 1])
                    units.append(Unit([m], [ab[:, kt, AV + side * HD:AV + (side + 1) * HD] for kt in key_tiles],
                                      both(normed, slice((h % 2) * HD, (h % 2 + 1) * HD), h // 2,
                                           slice(t * P, (t + 1) * P)), HD ** -0.5))
                for h in range(4):
                    maps = []
                    for m in range(2):
                        a = slice(m * HD, (m + 1) * HD)
                        maps.append(Map([(q2[a, 4 + h, t * P:(t + 1) * P], k2[a, 1 + h, keys])],
                                        [(len(key_tiles) * P, None)]))
                    units.append(Unit(maps, [ab[:, kt, BV + h * P:BV + (h + 1) * P] for kt in key_tiles],
                                      [y_b[:, h, t * P:(t + 1) * P]], HD ** -0.5, lam))
            return units

        class SubNorm(Stage):
            def __init__(self):
                self.av0, self.vv0, self.mm0 = take("av", 3), take("vv", 2), take("mm", 1)
                self.y = y_b.rearrange("p k t -> p (k t)")
                self.sq, self.r, self.fits = (arena[:, n:n + 2048] for n in (0, 2048, 4096))

            def tensor(self, pe):
                pe.wait_ge(av, self.av0 + 1)
                for h in range(4):
                    last = te.matmul(psum[:, h, :], ones, self.sq[:, h * 512:(h + 1) * 512], start=True, stop=True)
                last.then_inc(mm, 1)

            def scalar(self, act, step):
                se.activation(self.sq, self.y, ACT.Square, scale=2.0 ** -20).then_inc(av, 1)
                act.wait_ge(vv, self.vv0 + 1)
                se.activation(self.r, self.r, ACT.Sqrt).then_inc(av, 1)
                act.wait_ge(vv, self.vv0 + 2)
                se.copy(normed[0][:, 4:8, :].rearrange("p k t -> p (k t)"), self.y).then_inc(av, 1)

            def vector(self, dve, step):
                total = psum[:, 0:4, :].rearrange("p b n -> p (b n)")
                largest = float(np.finfo(np.float32).max) * 2.0 ** -40
                dve.wait_ge(mm, self.mm0 + 1)
                step(ve.tensor_scalar(self.r, total, 1.0 / P, EPS * 2.0 ** -40, ALU.mult, ALU.add))
                step(ve.tensor_scalar(self.fits, total, largest, None, ALU.is_le))
                ve.tensor_scalar(self.r, self.r, 2.0 ** 100, None, ALU.min).then_inc(vv, 1)
                dve.wait_ge(av, self.av0 + 2)
                step(ve.reciprocal(self.r, self.r))
                step(ve.scalar_tensor_tensor(out=self.r, in0=self.r, scalar=(1.0 - (0.8 - 0.6)) * 2.0 ** -20,
                                             in1=self.fits, op0=ALU.mult, op1=ALU.mult))
                ve.scalar_tensor_tensor(out=self.y, in0=self.y, scalar=col("b_sub"), in1=self.r,
                                        op0=ALU.mult, op1=ALU.mult).then_inc(vv, 1)
                dve.wait_ge(av, self.av0 + 3)
                hi, lo = (n[:, 4:8, :].rearrange("p k t -> p (k t)") for n in normed)
                ve.tensor_tensor(lo, self.y, hi.bitcast(F32), ALU.subtract)

        cdq = at(0, NT, 1280)
        cdk = at(2560, TT, 1280)
        kr = at(7680, TT, ROPE)
        dq_t = at(7808, 4, S)
        dk_t = at(8832, 4, 512)
        grid_bias = at(10880, 8, NT, S)
        space_grid = arena[:, 14976:14976 + 1536]
        cq_t = split_at("cq_t", (7808, 9344), 6, S)
        ckv_t = split_at("ckv_t", (10880, 11904), 2, 512)
        mq = at(12928, NT, 8 * MQ)
        kv = at(14464, TT, 1024)
        space_mla = arena[:, 18560:18560 + 2560]
        mk = at(0, TT, 8 * MQ)
        mq_t = at(3072, 8, S)
        mk_t = at(7808, 8, 512)

        def kr_projection():
            for t in range(TT):
                for k in range(KD):
                    for n in range(2):
                        te.matmul(psum[:, 0, t * ROPE:(t + 1) * ROPE], dt_x[n][:, k, t * P:(t + 1) * P], w_kr[:, k, :],
                                  start=(k == 0 and n == 0), stop=(k == KD - 1 and n == 1))

        def copy_kr(step):
            se.copy(kr.rearrange("p t n -> p (t n)"), psum[:, 0, 0:TT * ROPE])

        def spread_kr(step):
            for t in range(TT):
                ve.tensor_copy(heads_view(mk, 0, 8, ROPE, MQ, HD)(t), heads_view(kr, 0, 1, ROPE)(t).to_broadcast(
                    [P, 8, ROPE]))

        def grid_bias_stage():
            loads = []
            for t in range(NT):
                for rl in range(2):
                    for h in range(8):
                        dst = grid_bias[rl * GRID_W:(rl + 1) * GRID_W, h, t, :].rearrange("p (j k) -> p j k", j=ROWS)
                        start = (h * RPB_R + WIN_ROWS - 1 - 2 * t - rl) * RPB_PAD
                        loads.append((dst, bass.AP(scratch_rpb.tensor, start,
                                                   [[1, GRID_W], [RPB_PAD, ROWS], [1, GRID_W]])))
            return Mirror(grid_bias.rearrange("p h t n -> p (h t n)"), C("mirror64"), loads, C("colmask"))

        def grid_units():
            units = []
            for t in range(NT):
                for h in range(8):
                    a = slice((h % 2) * HD, (h % 2 + 1) * HD)
                    m = Map([(dq_t[a, h // 2, t * P:(t + 1) * P], dk_t[a, h // 2, :])],
                            [(S, grid_bias[:, h, t, :]), (S, None)])
                    units.append(Unit([m], [cdk[:, kt, 768 + h * HD:768 + (h + 1) * HD] for kt in range(TT)],
                                      both(normed, a, 4 + h // 2, slice(t * P, (t + 1) * P)), HD ** -0.5))
            return units

        def cq_turned(b):
            for m in range(2):
                last = se.activation(cq_t[0][:, 2 * b + m, :], psum[:, b, m * S:(m + 1) * S], ACT.Copy,
                                     scale=col("cq_norm", 2 * b + m))
            return last

        def cq_turned_lo(b):
            for m in range(2):
                last = ve.scalar_tensor_tensor(out=cq_t[1][:, 2 * b + m, :], in0=psum[:, b, m * S:(m + 1) * S],
                                               scalar=col("cq_norm", 2 * b + m),
                                               in1=cq_t[0][:, 2 * b + m, :].bitcast(F32),
                                               op0=ALU.mult, op1=ALU.subtract)
            return last

        def ckv_turned(b):
            return se.activation(ckv_t[0][:, b, :], psum[:, b, :], ACT.Copy, scale=col("ckv_norm", b))

        def ckv_turned_lo(b):
            return ve.scalar_tensor_tensor(out=ckv_t[1][:, b, :], in0=psum[:, b, :], scalar=col("ckv_norm", b),
                                           in1=ckv_t[0][:, b, :].bitcast(F32), op0=ALU.mult, op1=ALU.subtract)

        def mla_units():
            units = []
            for t in range(NT):
                for h in range(8):
                    m = Map([(mq_t[0:MQ, h, t * P:(t + 1) * P], mk_t[0:MQ, h, :])], [(2 * S, None)])
                    units.append(Unit([m], [kv[:, kt, h * P + HD:(h + 1) * P] for kt in range(TT)],
                                      both(normed, slice((h % 2) * HD, (h % 2 + 1) * HD), h // 2,
                                           slice(t * P, (t + 1) * P)), MQ ** -0.5))
            return units

        result = at(0, NT, D)

        class Store(Stage):
            def sync(self, sp):
                sp.wait_ge(stage_end, 3 * stages.index(self))
                sp.dma_start(out[0].rearrange("(t p) n -> p t n", p=P), result).then_inc(out_done, 16)
                sp.wait_ge(out_done, 16)

        stages = [Setup(), Conditions(), Modulation(0), Modulation(1)]
        stages += [
            Norm(S, lambda k, s: col("norm1", k), None),
            LinearF(W["w_qk"], KD, 24, normed, S, qk1),
            LinearT(W["w_v"], KD, AW // TW, normed, NT, v1),
            relative_bias(),
            Attention(attention1_units(), space1),
            ConvX(),
            LinearT(W["w_z"], KD, DI // TW, normed, NT, z1),
            Only("tensor", dt_projection),
            Only("vector", dt_bias),
            Only("scalar", dt_softplus),
            Only("vector", dt_decay),
            Only("tensor", sum_decay),
            Only("vector", negate_sums),
            Only("scalar", silu_conv), Only("scalar", silu_z),
            Turn([conv[:, 4 * (n // 4 % 4) + n % 4, (n // 16) * P:(n // 16 + 1) * P] for n in range(2 * KI)],
                 lambda b: se.copy(x_tok[:, b // 4, (b % 4) * 512:(b % 4 + 1) * 512], psum[:, b, :])),
            LinearF(W["w_g"], KD, 2 * KD, normed, S, gates1, ACT.Sigmoid),
            Only("tensor", cb_products),
            Only("scalar", copy_cb),
            Only("vector", scale_x),
            Scan(),
            Only("vector", mean_square),
            Only("scalar", inverse_root),
            Only("vector", normalise_groups),
            Turn([x_tok[:, t, k * P:(k + 1) * P] for k in range(KI) for t in range(NT)],
                 ssm_turned, ssm_turned_lo),
            Branches(),
            IntoResid(W["w_out"], KD, merged, S, None),
            Norm(S, lambda k, s: col("norm2", k), None),
            FfnUp(W["w_gu"], 0, S), IntoResid(W["w_down"][0:KD], KH, hidden, S, None),
            FfnUp(W["w_gu"], 1, S), IntoResid(W["w_down"][KD:2 * KD], KH, hidden, S, None),
            Norm(S, lambda k, s: col("final", k), None, in_place=True),
        ]
        every = 2 * S
        stages += [
            modulated(0, 0, 1, every), FfnUp(W["w_gu10"], 0, every), IntoResid(W["w_down10"][0:KD], KH, hidden, every, (0, 2)),
            FfnUp(W["w_gu10"], 1, every), IntoResid(W["w_down10"][KD:2 * KD], KH, hidden, every, (0, 2)),
            modulated(0, 3, 4, every),
            LinearT(W["w_ab"], KD, 2304 // TW, normed, TT, ab),
            HeadNorm([(heads_view(ab, start, heads, HD), TT, heads, HD, row(gain), rope64,
                       heads_view(ab, start, heads, HD))
                      for start, heads, gain in ((AQ, 8, "aq"), (BQ, 8, "bq"), (AK, 2, "ak"), (BK, 8, "bk"))], arena[:, 9216:15872]),
            Turn([ab[:, t, m * P:(m + 1) * P] for m in range(8) for t in range(TT)],
                 lambda b: se.copy(q2[:, b, :], psum[:, b, :])),
            Turn([ab[:, t, c:c + P] for c in (AK, *range(BK, BV, P)) for t in range(TT)],
                 lambda b: se.copy(k2[:, b, :], psum[:, b, :])),
            Only("vector", lambda_dots), Only("scalar", lambda_exp), Only("vector", lambda_sum),
            Attention(ab_units(), space_ab),
            SubNorm(),
            IntoResid(W["w_ab_out"], KD, normed, every, (0, 5)),
            modulated(0, 6, 7, every), FfnUp(W["w_gu20"], 0, every), IntoResid(W["w_down20"][0:KD], KH, hidden, every, (0, 8)),
            FfnUp(W["w_gu20"], 1, every), IntoResid(W["w_down20"][KD:2 * KD], KH, hidden, every, (0, 8)),
            modulated(1, 0, 1, every), FfnUp(W["w_gu11"], 0, every), IntoResid(W["w_down11"][0:KD], KH, hidden, every, (1, 2)),
            FfnUp(W["w_gu11"], 1, every), IntoResid(W["w_down11"][KD:2 * KD], KH, hidden, every, (1, 2)),
            modulated(1, 3, 4, every),
            LinearT(W["w_cdq"], KD, 1280 // TW, normed, NT, cdq),
            LinearT(W["w_cdk"], KD, 1280 // TW, normed, TT, cdk),
            Only("tensor", kr_projection), Only("scalar", copy_kr),
            HeadNorm([(heads_view(cdq, QR, 8, HD), NT, 8, HD, row("dq"), None, heads_view(cdq, QR, 8, HD)),
                      (heads_view(cdk, KVR, 8, HD), TT, 8, HD, row("dk"), None, heads_view(cdk, KVR, 8, HD)),
                      (heads_view(cdq, 0, 1, QR), NT, 1, QR, None, None, heads_view(cdq, 0, 1, QR)),
                      (heads_view(cdk, 0, 1, KVR), TT, 1, KVR, None, None, heads_view(cdk, 0, 1, KVR))],
                     arena[:, 10880:16512]),
            Turn([cdq[:, t, QR + m * P:QR + (m + 1) * P] for m in range(4) for t in range(NT)],
                 lambda b: se.copy(dq_t[:, 2 * b:2 * b + 2, :].rearrange("p m t -> p (m t)"), psum[:, b, :])),
            Turn([cdk[:, t, KVR + m * P:KVR + (m + 1) * P] for m in range(4) for t in range(TT)],
                 lambda b: se.copy(dk_t[:, b, :], psum[:, b, :])),
            grid_bias_stage(),
            Attention(grid_units(), space_grid),
            Turn([cdq[:, t, m * P:(m + 1) * P] for m in range(6) for t in range(NT)], cq_turned, cq_turned_lo),
            Turn([cdk[:, t, m * P:(m + 1) * P] for m in range(2) for t in range(TT)], ckv_turned, ckv_turned_lo),
            LinearT(W["w_uq"], QR // P, 3, cq_t, NT, mq),
            LinearT(W["w_ukv"], KVR // P, 4, ckv_t, TT, kv),
            HeadNorm([(heads_view(mq, 0, 8, HD, MQ), NT, 8, HD, row("cqn"), None, heads_view(mq, 0, 8, HD, MQ)),
                      (heads_view(mq, 0, 8, ROPE, MQ, HD), NT, 8, ROPE, row("cqr"), rope32,
                       heads_view(mq, 0, 8, ROPE, MQ, HD))], space_mla),
            HeadNorm([(heads_view(kv, 0, 8, HD, P), TT, 8, HD, row("ckn"), None, heads_view(mk, 0, 8, HD, MQ)),
                      ], space_mla),
            HeadNorm([(heads_view(kr, 0, 1, ROPE), TT, 1, ROPE, row("ckr"), rope32, heads_view(kr, 0, 1, ROPE))],
                     space_mla),
            Only("vector", spread_kr),
            Turn([mq[:, t, h * MQ:(h + 1) * MQ] for h in range(8) for t in range(NT)],
                 lambda b: se.copy(mq_t[0:MQ, 2 * b:2 * b + 2, :].rearrange("p m t -> p (m t)"), psum[0:MQ, b, :])),
            Turn([mk[:, t, h * MQ:(h + 1) * MQ] for h in range(8) for t in range(TT)],
                 lambda b: se.copy(mk_t[0:MQ, b, :], psum[0:MQ, b, :])),
            Attention(mla_units(), space_mla),
            IntoResid(W["w_cd_out"], KD, normed, S, (1, 5)),
            modulated(1, 6, 7, S), FfnUp(W["w_gu21"], 0, S), IntoResid(W["w_down21"][0:KD], KH, hidden, S, (1, 8)),
            FfnUp(W["w_gu21"], 1, S), IntoResid(W["w_down21"][KD:2 * KD], KH, hidden, S, (1, 8)),
            Turn([resid[:, k, t * P:(t + 1) * P] for t in range(NT) for k in range(KD)],
                 lambda b: se.copy(result[:, b // 2, (b % 2) * 512:(b % 2 + 1) * 512], psum[:, b, :])),
            Store(),
        ]

        streams = [st for st in stages if isinstance(st, Stream)]
        for st, following in zip(streams, streams[1:] + [None]):
            st.next = following

        def run(engine, name, step=None):
            for n, st in enumerate(stages):
                f = {"tensor": st.tensor, "scalar": st.scalar, "vector": st.vector}[name]
                f(engine, step) if step else f(engine)
                engine.drain().then_inc(stage_end, 1)
                engine.wait_ge(stage_end, 3 * (n + 1))

        @block.sync
        def _(sp):
            for st in stages:
                st.sync(sp)

        @block.tensor
        def _(pe):
            run(pe, "tensor")

        @block.scalar
        def _(act):
            run(act, "scalar", Steps(act, act_step))

        @block.vector
        def _(dve):
            run(dve, "vector", Steps(dve, dve_step))



def chunked(w, width, rows):
    k, m = w.shape
    a = w.reshape(k // (rows * P), rows, P, m // width, width)
    return a.transpose(3, 0, 2, 1, 4).reshape(-1, P, rows * width)


def f_chunks(w):
    return chunked(w, FW, w.shape[0] // P)


def t_chunks(w):
    return chunked(w, TW, w.shape[0] // P // 2)


def down_chunks(w):
    return np.concatenate([f_chunks(w[:FF // 2]), f_chunks(w[FF // 2:])])


def feature_major(v):
    return v.reshape(-1, P).T


def lay_out(x):
    w_in = x["w_in"][0]
    cuts = np.cumsum([AW, AW, AW, DI, XBC, SH, 2 * D])
    wq, wk, wv, wz, wx, wdt, wg = (w_in[:, a:b] for a, b in zip([0, *cuts[:-1]], cuts))
    cd = x["cd_w_in_2"][0]
    cc = np.cumsum([QR, 512, KVR, ROPE, 512, 512])
    c_q, c_dq, c_kv, c_kr, c_dk, c_dv = (cd[:, a:b] for a, b in zip([0, *cc[:-1]], cc))
    ab = x["ab_w_in_2"][0]
    aq = ab[:, :512].reshape(D, 2, 4, HD).transpose(0, 2, 1, 3).reshape(D, 512)
    ab = np.concatenate([aq, ab[:, 512:]], 1)
    gate1, up1 = f_chunks(x["w_ffn_in"][0][:, :FF]), f_chunks(x["w_ffn_in"][0][:, FF:])

    def alternate(a, b):
        return np.stack([a, b], 1).reshape(2 * a.shape[0], *a.shape[1:])

    a, s = x["w_attn_branch"][0], x["w_ssm_branch"][0]
    branch = chunked(np.concatenate([a, s], 0), FW, 10)
    out = {
        "x": x["x"][0].T.reshape(KD, P, S).transpose(1, 0, 2),
        "ctx": x["ctx_2"][0].T.reshape(KD, P, S).transpose(1, 0, 2),
        "w_qk": np.concatenate([f_chunks(wq), f_chunks(wk)]), "w_v": t_chunks(wv), "w_z": t_chunks(wz),
        "w_x": f_chunks(wx), "w_g": f_chunks(wg),
        "w_dt": wdt.reshape(KD, P, SH).transpose(1, 0, 2),
        "w_kr": c_kr.reshape(KD, P, ROPE).transpose(1, 0, 2),
        "w_branch": branch, "w_out": f_chunks(x["w_out"][0]),
        "w_gu": alternate(gate1, up1), "w_down": down_chunks(x["w_ffn_out"][0]),
        "w_mod": np.concatenate([t_chunks(w) for w in x["w_mod_2"]]),
        "w_ab": t_chunks(ab), "w_ab_out": f_chunks(x["ab_w_out_2"][0]),
        "w_cdq": np.concatenate([t_chunks(c_q), t_chunks(c_dq)]),
        "w_cdk": np.concatenate([t_chunks(c_kv), t_chunks(c_dk), t_chunks(c_dv)]),
        "w_uq": t_chunks(x["c_w_uq_2"][0]), "w_ukv": t_chunks(x["c_w_ukv_2"][0]),
        "w_cd_out": f_chunks(x["cd_w_out_2"][0]),
        "rel_bias": x["rel_bias"], "rpb": x["d_rpb_2"][0].reshape(8 * RPB_R, RPB_C),
    }
    for n in (1, 2):
        for layer in range(LAYERS):
            out[f"w_gu{n}{layer}"] = alternate(f_chunks(x[f"ffn{n}_w_gate_2"][layer]),
                                               f_chunks(x[f"ffn{n}_w_up_2"][layer]))
            out[f"w_down{n}{layer}"] = down_chunks(x[f"ffn{n}_w_down_2"][layer])
    cond = np.stack([feature_major(x["c_2"][0]), feature_major(x["c_ctx_2"])], 2).reshape(P, 2 * KD)
    vectors = {
        "norm1": feature_major(x["norm1_w"][0]), "norm2": feature_major(x["norm2_w"][0]),
        "final": feature_major(x["final_norm_w"]),
        "conv_w": np.concatenate([feature_major(r) for r in x["conv_w"][0]], 1),
        "conv_b": feature_major(x["conv_b"][0]), "ssm_norm": feature_major(x["ssm_norm_w"][0]),
        "b_mod": feature_major(x["b_mod_2"].reshape(-1)), "cond": cond, "b_sub": feature_major(x["b_sub_norm_2"][0]),
        "cq_norm": feature_major(x["c_q_a_norm_2"][0]), "ckv_norm": feature_major(x["c_kv_a_norm_2"][0]),
    }
    out["cols"] = np.concatenate([vectors[n] for n in COLS], 1)
    names = ("dt_bias", "a_log", "d_skip", "a_q_norm_2", "a_k_norm_2", "b_q_norm_2", "b_k_norm_2", "d_q_norm_2",
             "d_k_norm_2", "c_q_nope_norm_2", "c_q_rope_norm_2", "c_k_nope_norm_2", "c_k_rope_norm_2", "a_sink_2",
             "b_lambda_q1_2", "b_lambda_k1_2", "b_lambda_q2_2", "b_lambda_k2_2")
    out["rowv"] = np.concatenate([x[n][0] for n in names])[None]
    return out


def kernel(**inputs):
    import concourse.bacc as bacc
    from concourse.bass_utils import run_bass_kernel_spmd

    nc = bacc.Bacc("TRN2", target_bir_lowering=False, num_devices=1, dynamic_dma_scratch_size=1024)
    laid = lay_out({name: np.asarray(a) for name, a in inputs.items()})
    consts, where = shape_constants()
    laid["consts"] = consts
    arrays = {"in_" + name: np.ascontiguousarray(a) for name, a in laid.items()}
    W = {name: nc.dram_tensor("in_" + name, a.shape, F32, kind="ExternalInput").ap() for name, a in laid.items()}
    out = nc.dram_tensor("out_0", (1, S, D), F32, kind="ExternalOutput").ap()
    build(nc, W, W["consts"], where, out)
    r = run_bass_kernel_spmd(nc, [arrays], core_ids=[0])
    return r.results[0]["out_0"]
```
